# Optimizing a Trainium2 kernel written in Bass

```python
import jax, jax.numpy as jnp
from jax import lax
import numpy as np

D_MODEL = 1024
BATCH = 1
SEQ = 256
DEPTH = 1
DEC_BATCH = 8
DEC_SEQ = 1
PAST_LEN = 2048
PAGE_SIZE = 128

LRU_WIDTH = D_MODEL
LRU_BLOCKS = 8
LRU_BLOCK = LRU_WIDTH // LRU_BLOCKS
CONV_WIDTH = 4
LRU_C = 8.0
RET_HEADS = 4
RET_DK = D_MODEL // RET_HEADS
RET_DV = 2 * RET_DK
RET_CHUNK = 128
ROPE_BASE = 10000.0
MEM_TOKENS = 256
MEM_HEADS = 4
MEM_DH = D_MODEL // MEM_HEADS
N_GROUPS = 4
EXP_PER_GROUP = 8
N_EXPERTS = N_GROUPS * EXP_PER_GROUP
EXP_FF = 512
TOP_K_IN_GROUP = 2

N_BRANCHES = 3
EPS = 1e-6
SPLITS = (LRU_WIDTH, LRU_WIDTH, RET_HEADS * RET_DK, RET_HEADS * RET_DK,
          RET_HEADS * RET_DV, RET_HEADS * RET_DV, MEM_HEADS * MEM_DH, N_BRANCHES * D_MODEL)
IN_WIDTH = sum(SPLITS)

kernel_name = 'hybrid_rglru_retention_memxattn_hmoe_step'

def split_points():
    pts = []
    acc = 0
    for s in SPLITS[:-1]:
        acc += s
        pts.append(acc)
    return pts

def rmsnorm(x, g):
    xf = x.astype(jnp.float32)
    y = xf * lax.rsqrt(jnp.mean(xf * xf, axis=-1, keepdims=True) + EPS)
    return (y * g.astype(jnp.float32)).astype(x.dtype)

def rotary(x, pos):
    half = x.shape[-1] // 2
    inv = ROPE_BASE ** (-jnp.linspace(0.0, 1.0, half, dtype=jnp.float32))
    ang = pos.astype(jnp.float32)[:, None] * inv[None, :]
    cos = jnp.cos(ang)[None, :, None, :]
    sin = jnp.sin(ang)[None, :, None, :]
    x1, x2 = x[..., :half], x[..., half:]
    return jnp.concatenate([x1 * cos - x2 * sin, x2 * cos + x1 * sin], axis=-1)

def causal_conv(x, prev, w, b):
    length = x.shape[1]
    xp = jnp.concatenate([prev.astype(x.dtype), x], axis=1)
    y = b
    for j in range(CONV_WIDTH):
        y = y + w[j] * xp[:, j:j + length]
    return y, xp[:, -(CONV_WIDTH - 1):]

def linear_scan(a, b, h0):
    b = b.at[:, 0].add(a[:, 0] * h0)

    def combine(left, right):
        return left[0] * right[0], right[0] * left[1] + right[1]

    _, h = lax.associative_scan(combine, (a, b), axis=1)
    return h

def rg_lru(x, pos, h0, w_r, b_r, w_i, b_i, lam):
    f32 = jnp.float32
    bsz, length, width = x.shape
    xb = x.reshape(bsz, length, LRU_BLOCKS, LRU_BLOCK)
    r = jax.nn.sigmoid(jnp.einsum('blnc,ncd->blnd', xb, w_r).reshape(bsz, length, width).astype(f32) + b_r.astype(f32))
    i = jax.nn.sigmoid(jnp.einsum('blnc,ncd->blnd', xb, w_i).reshape(bsz, length, width).astype(f32) + b_i.astype(f32))
    log_a = -LRU_C * r * jax.nn.softplus(-lam.astype(f32))
    a = jnp.exp(log_a)
    mult = jnp.sqrt(-jnp.expm1(2.0 * log_a))
    mult = jnp.where((pos == 0)[None, :, None], 1.0, mult)
    h = linear_scan(a, mult * i * x.astype(f32), h0.astype(f32))
    return h, h[:, -1]

def retention(q, k, v, s0):
    bsz, length = q.shape[0], q.shape[1]
    c = RET_CHUNK if length % RET_CHUNK == 0 else length
    nc = length // c
    log_g = jnp.log1p(-(2.0 ** (-5.0 - jnp.arange(RET_HEADS, dtype=jnp.float32))))
    n = jnp.arange(c, dtype=jnp.float32)
    diff = n[:, None] - n[None, :]
    dmask = jnp.where(diff[None] >= 0, jnp.exp(jnp.maximum(diff, 0.0)[None] * log_g[:, None, None]), 0.0)
    q_decay = jnp.exp((n[None, :] + 1.0) * log_g[:, None])
    k_decay = jnp.exp((c - 1.0 - n[None, :]) * log_g[:, None])
    s_decay = jnp.exp(c * log_g)

    def to_chunks(t):
        return t.reshape(bsz, nc, c, RET_HEADS, t.shape[-1]).transpose(1, 0, 3, 2, 4)

    def step(s, inp):
        qc, kc, vc = inp
        att = jnp.einsum('bhnk,bhmk->bhnm', qc, kc) * dmask
        o = (jnp.einsum('bhnm,bhmv->bhnv', att, vc)
             + jnp.einsum('bhnk,bhkv->bhnv', qc * q_decay[..., None], s))
        s = s * s_decay[:, None, None] + jnp.einsum('bhmk,bhmv->bhkv', kc * k_decay[..., None], vc)
        return s, o

    s_last, o = lax.scan(step, s0, (to_chunks(q), to_chunks(k), to_chunks(v)))
    o = o.transpose(1, 0, 3, 2, 4).reshape(bsz, length, RET_HEADS, RET_DV)
    return o, s_last

def hier_moe(x, w_grp, b_grp, w_exp_router, b_exp_router, w_gate, w_up, w_down):
    f32 = jnp.float32
    t = x.shape[0]
    grp_logits = (x @ w_grp).astype(f32) + b_grp.astype(f32)
    grp_prob = jax.nn.softmax(grp_logits, axis=-1)
    g_idx = jnp.argmax(grp_logits, axis=-1)
    g_val = jnp.take_along_axis(grp_prob, g_idx[:, None], axis=-1)
    exp_logits = jnp.einsum('td,gde->tge', x, w_exp_router).astype(f32) + b_exp_router.astype(f32)
    exp_logits = jnp.take_along_axis(exp_logits, g_idx[:, None, None], axis=1)[:, 0]
    exp_prob = jax.nn.softmax(exp_logits, axis=-1)
    top_v, top_i = lax.top_k(exp_prob, TOP_K_IN_GROUP)
    top_w = g_val * top_v / jnp.sum(top_v, axis=-1, keepdims=True)
    flat = g_idx[:, None].astype(jnp.int32) * EXP_PER_GROUP + top_i
    dense_w = jnp.sum(jax.nn.one_hot(flat, N_EXPERTS, dtype=f32) * top_w[..., None], axis=1)
    dense_w = dense_w.astype(x.dtype).reshape(t, N_GROUPS, EXP_PER_GROUP)
    y = jnp.zeros_like(x)
    for gi in range(N_GROUPS):
        hid = jax.nn.silu(jnp.einsum('td,edf->tef', x, w_gate[gi])) * jnp.einsum('td,edf->tef', x, w_up[gi])
        y = y + jnp.einsum('tef,efd->td', hid * dense_w[:, gi, :, None], w_down[gi])
    return y

def layer_step(x, pos, conv_prev, h_prev, s_prev, mem_k, mem_v, lp):
    f32 = jnp.float32
    bsz, length, _ = x.shape
    dt = x.dtype
    xn = rmsnorm(x, lp['norm_mix'])
    z = xn @ lp['w_in']
    u_x, u_y, q, k, v, g, mq, gates = jnp.split(z, split_points(), axis=-1)
    u_c, conv_new = causal_conv(u_x, conv_prev, lp['conv_w'], lp['conv_b'])
    h, h_last = rg_lru(u_c, pos, h_prev, lp['w_r'], lp['b_r'], lp['w_i'], lp['b_i'], lp['lru_lambda'])
    a_out = (h.astype(dt) * jax.nn.gelu(u_y)) @ lp['w_branch_lru']
    qh = rotary(q.reshape(bsz, length, RET_HEADS, RET_DK).astype(f32), pos)
    kh = rotary(k.reshape(bsz, length, RET_HEADS, RET_DK).astype(f32), pos) * (RET_DK ** -0.5)
    vh = v.reshape(bsz, length, RET_HEADS, RET_DV).astype(f32)
    o, s_new = retention(qh, kh, vh, s_prev.astype(f32))
    o = o * lax.rsqrt(jnp.mean(o * o, axis=-1, keepdims=True) + EPS)
    b_out = (jax.nn.silu(g) * o.reshape(bsz, length, RET_HEADS * RET_DV).astype(dt)) @ lp['w_branch_ret']
    mqh = mq.reshape(bsz, length, MEM_HEADS, MEM_DH)
    logits = jnp.einsum('blhd,bmhd->bhlm', mqh, mem_k).astype(f32) * (MEM_DH ** -0.5)
    p = jax.nn.softmax(logits, axis=-1).astype(dt)
    c = jnp.einsum('bhlm,bmhd->blhd', p, mem_v).reshape(bsz, length, MEM_HEADS * MEM_DH)
    c_out = c @ lp['w_branch_mem']
    g_a, g_b, g_c = jnp.split(gates, N_BRANCHES, axis=-1)
    merged = jax.nn.sigmoid(g_a) * a_out + jax.nn.sigmoid(g_b) * b_out + jax.nn.sigmoid(g_c) * c_out
    x = x + merged @ lp['w_out']
    xn2 = rmsnorm(x, lp['norm_ffn']).reshape(bsz * length, D_MODEL)
    ffn = hier_moe(xn2, lp['w_grp'], lp['b_grp'], lp['w_exp_router'], lp['b_exp_router'],
                   lp['w_gate'], lp['w_up'], lp['w_down'])
    x = x + ffn.reshape(bsz, length, D_MODEL)
    return x, conv_new, h_last, s_new

def setup_inputs(seed: int = 0) -> dict:
    key = jax.random.key(seed)
    ks = jax.random.split(key, 40)
    f32 = jnp.float32

    def nrm(k, shape, scale):
        return jax.random.normal(k, shape, f32) * scale

    u = jax.random.uniform(ks[39], (DEPTH, LRU_WIDTH), f32, 0.9, 0.999)
    sig = u ** (1.0 / LRU_C)
    lam = jnp.log(sig) - jnp.log1p(-sig)
    return {
        'x_prompt': nrm(ks[0], (BATCH, SEQ, D_MODEL), 1.0),
        'x_sample': nrm(ks[1], (DEC_BATCH, DEC_SEQ, D_MODEL), 1.0),
        'mem_prompt': nrm(ks[2], (BATCH, MEM_TOKENS, D_MODEL), 1.0),
        'state_conv': nrm(ks[3], (DEPTH, DEC_BATCH, CONV_WIDTH - 1, LRU_WIDTH), 1.0),
        'state_lru': nrm(ks[4], (DEPTH, DEC_BATCH, LRU_WIDTH), 0.5),
        'state_ret': nrm(ks[5], (DEPTH, DEC_BATCH, RET_HEADS, RET_DK, RET_DV), 0.5),
        'cache_mem_k': nrm(ks[6], (DEPTH, DEC_BATCH, MEM_TOKENS, MEM_HEADS, MEM_DH), 1.0),
        'cache_mem_v': nrm(ks[7], (DEPTH, DEC_BATCH, MEM_TOKENS, MEM_HEADS, MEM_DH), 1.0),
        'norm_mix': 1.0 + nrm(ks[8], (DEPTH, D_MODEL), 0.05),
        'norm_ffn': 1.0 + nrm(ks[9], (DEPTH, D_MODEL), 0.05),
        'norm_mem': 1.0 + nrm(ks[10], (DEPTH, D_MODEL), 0.05),
        'norm_final': 1.0 + nrm(ks[11], (D_MODEL,), 0.05),
        'w_in': nrm(ks[12], (DEPTH, D_MODEL, IN_WIDTH), D_MODEL ** -0.5),
        'w_mem_kv': nrm(ks[13], (DEPTH, D_MODEL, 2 * MEM_HEADS * MEM_DH), D_MODEL ** -0.5),
        'conv_w': nrm(ks[14], (DEPTH, CONV_WIDTH, LRU_WIDTH), CONV_WIDTH ** -0.5),
        'conv_b': nrm(ks[15], (DEPTH, LRU_WIDTH), 0.01),
        'w_r': nrm(ks[16], (DEPTH, LRU_BLOCKS, LRU_BLOCK, LRU_BLOCK), LRU_BLOCK ** -0.5),
        'b_r': nrm(ks[17], (DEPTH, LRU_WIDTH), 0.01),
        'w_i': nrm(ks[18], (DEPTH, LRU_BLOCKS, LRU_BLOCK, LRU_BLOCK), LRU_BLOCK ** -0.5),
        'b_i': nrm(ks[19], (DEPTH, LRU_WIDTH), 0.01),
        'lru_lambda': lam,
        'w_branch_lru': nrm(ks[20], (DEPTH, LRU_WIDTH, D_MODEL), LRU_WIDTH ** -0.5),
        'w_branch_ret': nrm(ks[21], (DEPTH, RET_HEADS * RET_DV, D_MODEL), (RET_HEADS * RET_DV) ** -0.5),
        'w_branch_mem': nrm(ks[22], (DEPTH, MEM_HEADS * MEM_DH, D_MODEL), (MEM_HEADS * MEM_DH) ** -0.5),
        'w_out': nrm(ks[23], (DEPTH, D_MODEL, D_MODEL), D_MODEL ** -0.5),
        'w_grp': nrm(ks[24], (DEPTH, D_MODEL, N_GROUPS), D_MODEL ** -0.5),
        'b_grp': nrm(ks[25], (DEPTH, N_GROUPS), 0.01),
        'w_exp_router': nrm(ks[26], (DEPTH, N_GROUPS, D_MODEL, EXP_PER_GROUP), D_MODEL ** -0.5),
        'b_exp_router': nrm(ks[27], (DEPTH, N_GROUPS, EXP_PER_GROUP), 0.01),
        'w_gate': nrm(ks[28], (DEPTH, N_GROUPS, EXP_PER_GROUP, D_MODEL, EXP_FF), D_MODEL ** -0.5),
        'w_up': nrm(ks[29], (DEPTH, N_GROUPS, EXP_PER_GROUP, D_MODEL, EXP_FF), D_MODEL ** -0.5),
        'w_down': nrm(ks[30], (DEPTH, N_GROUPS, EXP_PER_GROUP, EXP_FF, D_MODEL), EXP_FF ** -0.5),
    }

def reference(x_prompt, x_sample, mem_prompt, state_conv, state_lru, state_ret, cache_mem_k, cache_mem_v,
              norm_mix, norm_ffn, norm_mem, norm_final, w_in, w_mem_kv, conv_w, conv_b, w_r, b_r, w_i, b_i,
              lru_lambda, w_branch_lru, w_branch_ret, w_branch_mem, w_out, w_grp, b_grp, w_exp_router,
              b_exp_router, w_gate, w_up, w_down):
    f32 = jnp.float32
    bp, lp_len = x_prompt.shape[0], x_prompt.shape[1]
    pos_p = jnp.arange(lp_len, dtype=jnp.int32)
    pos_s = PAST_LEN + jnp.arange(x_sample.shape[1], dtype=jnp.int32)
    yp, ys = x_prompt, x_sample
    conv_p, lru_p, ret_p, mk_p, mv_p = [], [], [], [], []
    conv_s, lru_s, ret_s = [], [], []
    for layer in range(DEPTH):
        lp = {
            'norm_mix': norm_mix[layer], 'norm_ffn': norm_ffn[layer], 'w_in': w_in[layer],
            'conv_w': conv_w[layer], 'conv_b': conv_b[layer], 'w_r': w_r[layer], 'b_r': b_r[layer],
            'w_i': w_i[layer], 'b_i': b_i[layer], 'lru_lambda': lru_lambda[layer],
            'w_branch_lru': w_branch_lru[layer], 'w_branch_ret': w_branch_ret[layer],
            'w_branch_mem': w_branch_mem[layer], 'w_out': w_out[layer], 'w_grp': w_grp[layer],
            'b_grp': b_grp[layer], 'w_exp_router': w_exp_router[layer], 'b_exp_router': b_exp_router[layer],
            'w_gate': w_gate[layer], 'w_up': w_up[layer], 'w_down': w_down[layer],
        }
        mkv = rmsnorm(mem_prompt, norm_mem[layer]) @ w_mem_kv[layer]
        mk, mv = jnp.split(mkv, 2, axis=-1)
        mk = mk.reshape(bp, MEM_TOKENS, MEM_HEADS, MEM_DH)
        mv = mv.reshape(bp, MEM_TOKENS, MEM_HEADS, MEM_DH)
        conv0 = jnp.zeros((bp, CONV_WIDTH - 1, LRU_WIDTH), x_prompt.dtype)
        h0 = jnp.zeros((bp, LRU_WIDTH), f32)
        s0 = jnp.zeros((bp, RET_HEADS, RET_DK, RET_DV), f32)
        yp, c_new, h_new, s_new = layer_step(yp, pos_p, conv0, h0, s0, mk, mv, lp)
        conv_p.append(c_new); lru_p.append(h_new); ret_p.append(s_new); mk_p.append(mk); mv_p.append(mv)
        ys, c_new, h_new, s_new = layer_step(ys, pos_s, state_conv[layer], state_lru[layer], state_ret[layer],
                                             cache_mem_k[layer], cache_mem_v[layer], lp)
        conv_s.append(c_new); lru_s.append(h_new); ret_s.append(s_new)
    yp = rmsnorm(yp, norm_final)
    ys = rmsnorm(ys, norm_final)
    dp, ds = x_prompt.dtype, state_ret.dtype
    return (yp, ys,
            jnp.stack(conv_p).astype(dp), jnp.stack(lru_p).astype(dp), jnp.stack(ret_p).astype(dp),
            jnp.stack(mk_p).astype(dp), jnp.stack(mv_p).astype(dp),
            jnp.stack(conv_s).astype(state_conv.dtype), jnp.stack(lru_s).astype(state_lru.dtype),
            jnp.stack(ret_s).astype(ds))


_drawn_inputs = setup_inputs


def setup_inputs(seed=0):
    import zlib

    import numpy as np

    out = dict(_drawn_inputs(seed))
    spreads = {}
    factors = {'b_r': 23.69, 'b_i': 8.0, 'b_grp': 5.524, 'b_exp_router': 3.964}
    for name, (base, spread) in spreads.items():
        noise = np.random.default_rng([zlib.crc32(name.encode()), seed]).standard_normal(out[name].shape)
        drawn = base * np.exp(spread * noise) if base else spread * noise
        out[name] = __import__('jax').numpy.asarray(drawn.astype(out[name].dtype))
    for name, factor in factors.items():
        out[name] = (out[name] * factor).astype(out[name].dtype)
    return out
```

```python
from contextlib import ExitStack

import numpy as np
import concourse.bass as bass
from concourse import mybir

F32 = mybir.dt.float32
BF16 = mybir.dt.bfloat16
I32 = mybir.dt.int32
ACT = mybir.ActivationFunctionType
ALU = mybir.AluOpType
AX = mybir.AxisListType

P = 128
D = 1024
KT = D // P
TP, NS = 256, 8
T = TP + NS
HEADS, DK, DV = 4, 256, 512
VT = HEADS * DV // P
EPS = 1e-6
EXPERTS, GROUPS, PER_GROUP, FF = 32, 4, 8, 512
NLOG = GROUPS + EXPERTS
SLOTS = 64
OVER = (2 * T) // (SLOTS + 1)
COLS = EXPERTS + OVER
TT = 3
CHUNK = 2048
RING = 6
RING1 = 5
GAMMA = [float(1.0 - 2.0 ** (-5.0 - h)) for h in range(HEADS)]
PAST_LEN = 2048
ROPE_BASE = 10000.0

OFF = {"ux": 0, "uy": 1024, "q": 2048, "k": 3072, "v": 4096, "g": 6144, "mq": 8192,
       "ga": 9216, "gb": 10240, "gc": 11264}
CH = {n: i for i, n in enumerate(["norm_mix", "norm_ffn", "norm_mem", "norm_final", "conv_b", "b_r", "b_i",
                                  "lam", "w0", "w1", "w2", "w3"])}


def shape_constants():
    f = np.float32
    half = DK // 2
    inv = np.power(f(ROPE_BASE), -np.linspace(0.0, 1.0, half, dtype=f)).astype(f)
    pos = np.concatenate([np.arange(TP), np.full(NS, PAST_LEN)]).astype(f)
    ang = (inv[:, None] * pos[None, :]).astype(f)
    log_g = np.log1p(-(2.0 ** (-5.0 - np.arange(HEADS))))
    p = np.arange(P)
    mask = np.zeros((P, HEADS, 384))
    for h in range(HEADS):
        n = np.arange(TP)
        mask[:, h, :TP] = np.where(n[None] >= p[:, None], np.exp(np.maximum(n[None] - p[:, None], 0) * log_g[h]), 0)
        mask[:, h, TP:] = mask[:, h, :P]
    kdec = np.zeros((P, 2, HEADS))
    for mt in range(2):
        kdec[:, mt, :] = np.exp((TP - 1 - (mt * P + p))[:, None] * log_g[None])
    valid = np.ones((P, TT))
    valid[T - 2 * P:, 2] = 0
    parts = {
        "cos": np.cos(ang), "sin": np.sin(ang), "dmask": mask.reshape(P, -1),
        "ident": np.eye(P), "kdec": kdec.reshape(P, -1), "before": (p[:, None] < p[None, :]).astype(f), "valid": valid,
        "slot2": np.tile(np.arange(SLOTS), (P, 2)), "count32": np.tile(np.arange(EXPERTS), (P, 1)),
        "count8": np.tile(np.arange(OVER), (P, 1)),
    }
    at, cols, off = {}, [], 0
    for name, a in parts.items():
        at[name] = (off, off + a.shape[1])
        off += a.shape[1]
        cols.append(a.astype(f))
    return np.ascontiguousarray(np.concatenate(cols, axis=1)), at


STAGES = ["load", "mem", "mq", "ux", "uy", "q", "k", "v", "rows", "ga", "gc", "gb", "g", "ret", "x2", "route", "moe",
          "end"]
ARENA = 53192
NCONST = shape_constants()[0].shape[1]
NROPE, NMASK = 2 * T, HEADS * 384
BUFFERS = {
    "rope": (NROPE, "load", "v"),
    "dmask": (NMASK, "load", "gc"),
    "const": (NCONST - NROPE - NMASK, "load", "end"),
    "ones": (P, "load", "end"),
    "chan": (12 * KT, "load", "end"),
    "xT": (KT * T, "load", "mem"),
    "x": (KT * T, "gb", "end"),
    "xnT": (KT * T, "load", "route"),
    "rstd": (2 * T, "load", "end"),
    "small": (KT * 8, "load", "q"),
    "sp4": (KT, "load", "q"),
    "brh": (2 * KT, "load", "q"),
    "stats": (64, "load", "v"),
    "eps_col": (8, "load", "end"),
    "memT": (KT * TP, "load", "mem"),
    "sq": (KT * T, "load", "mem"),
    "wr": (KT * P, "load", "q"),
    "wi": (KT * P, "load", "q"),
    "sconv": (KT * 3 * NS, "load", "uy"),
    "slru": (KT * NS, "load", "v"),
    "mk_rows": (2 * D, "mem", "mq"),
    "mv_rows": (2 * D, "mem", "uy"),
    "mkT": (KT * TP, "mem", "uy"),
    "mqT": (KT * T, "mq", "uy"),
    "mqs_rows": (D, "mq", "k"),
    "mq_row0": (D, "mq", "k"),
    "qb": (2 * D, "mq", "k"),
    "kv": (2 * 2 * D, "mq", "v"),
    "prod": (2 * D, "mq", "k"),
    "L": (64, "mq", "k"),
    "prob": (4 * TP, "ux", "uy"),
    "probT": (2 * TP, "ux", "uy"),
    "cT": (KT * T, "ux", "gc"),
    "uxp": (KT * 272, "ux", "uy"),
    "uc": (KT * T, "uy", "v"),
    "convt": (64, "uy", "uy"),
    "Tr": (KT * T, "q", "rows"),
    "Ti": (KT * T, "q", "rows"),
    "Rb": (KT * T, "q", "v"),
    "uyT": (KT * T, "uy", "ga"),
    "lru_st": (KT * 16, "ux", "end"),
    "conv_st": (KT * 16, "ux", "end"),
    "qT": (KT * T, "q", "gc"),
    "kT": (KT * T, "k", "gc"),
    "rtmp": (HEADS * 2 * T, "k", "v"),
    "vT": (VT * T, "v", "rows"),
    "v_rows": (2 * HEADS * DV, "rows", "gc"),
    "k_rows": (2 * D, "v", "gc"),
    "vs_rows": (HEADS * DV, "rows", "gc"),
    "v_row0": (D, "rows", "gc"),
    "vb": (2 * D, "rows", "gc"),
    "st": (3 * 4 * DV, "rows", "gc"),
    "p32": (TP, "k", "k"),
    "PM": (512, "k", "v"),
    "cs": (TP, "k", "rows"),
    "QM": (KT * 64, "k", "gc"),
    "attT": (384, "ga", "gc"),
    "oT": (VT * T, "ga", "ret"),
    "S_st": (2 * DV, "ga", "gb"),
    "os": (DV, "ga", "gb"),
    "merged": (KT * T, "ga", "x2"),
    "tgate": (KT * T, "gc", "x2"),
    "gt": (2 * T, "g", "g"),
    "sq2": (4 * T, "gb", "gb"),
    "sq3": (KT * T, "route", "end"),
    "rout": (KT * NLOG, "load", "end"),
    "rbias": (NLOG, "load", "end"),
    "xr0": (TT * D // 2, "route", "end"),
    "xr1": (TT * D // 2, "route", "end"),
    "xr2": (TT * D // 2, "route", "end"),
    "xres": (512, "route", "end"),
    "lgt": (TT * NLOG, "route", "end"),
    "Rc": (TT * COLS, "route", "end"),
    "Wc": (TT * COLS, "route", "end"),
    "M01": (TT * EXPERTS, "route", "end"),
    "tmpA": (TT * OVER * EXPERTS, "route", "end"),
    "tmpB": (TT * 64, "route", "end"),
    "tmpC": (TT * 64, "route", "end"),
    "tmpD": (TT * 64, "route", "end"),
    "ov": (512, "route", "end"),
    "ints": (16, "route", "end"),
    "eq": (TT * P, "route", "end"),
    "Sw": (2 * TT * P, "route", "end"),
    "Sb": (TT * SLOTS, "route", "end"),
    "XgT": (2 * KT * SLOTS, "route", "end"),
    "SwT": (2 * T, "route", "end"),
    "tg": (256, "route", "end"),
    "hid": (256, "route", "end"),
    "hT": (256, "route", "end"),
    "yS": (2 * D, "route", "end"),
    "acc": (KT * T, "route", "end"),
    "tmid": (256, "route", "end"),
    "zero_row": (D, "route", "end"),
    "hid_z": (8, "route", "end"),
}


def place_buffers():
    stage = {s: i for i, s in enumerate(STAGES)}

    def place(power):
        held = [(0, RING1 * CHUNK, 0, stage["end"]), (RING1 * CHUNK, 2 * RING * CHUNK, stage["ret"], stage["end"])]
        found = {}
        for name, (size, first, last) in sorted(
                BUFFERS.items(), key=lambda x: -x[1][0] * (stage[x[1][2]] - stage[x[1][1]] + 1) ** power):
            a, b, at = stage[first], stage[last], 0
            size = (size + 7) // 8 * 8
            for lo, hi, x, y in sorted(held):
                if b < x or y < a or hi <= at:
                    continue
                if lo >= at + size:
                    break
                at = hi
            held.append((at, at + size, a, b))
            found[name] = at
        return found, max(h[1] for h in held)

    found, top = min((place(n / 20) for n in range(61)), key=lambda x: x[1])
    assert top <= ARENA, top
    return found


def weave(main, side):
    out, n = [], 0
    for i, m in enumerate(main):
        out.append(m)
        while n * len(main) < (i + 1) * len(side):
            out.append(side[n])
            n += 1
    return out


def tensor_order():
    t = lambda kind, n: [(kind, i) for i in range(n)]
    heads = range(HEADS)
    lg = [[("lg", h, 0), ("lg", h, 1)] for h in heads]
    pv = [[("pT", h), ("pv", h, 0), ("pv", h, 1)] for h in heads]
    attn = lg[0] + lg[1] + pv[0] + lg[2] + pv[1] + lg[3] + pv[2] + pv[3]
    gates = [x for n in range(KT) for x in (("r", n), ("i", n))]
    kl = t("kl", NS)
    cache = [("sl",), ("spT",)] + t("sc", NS)
    krows = [("kr", m, q) for m in range(2) for q in range(2)]
    v = t("v", VT)
    vrows = t("vs", 4) + [("vr", m, q) for q in range(4) for m in range(2)]
    ret = []
    for h in heads:
        ret += [("att", h)] + [("o", h, j) for j in range(4)] + [("S", h, i) for i in range(2)]
    so = [("sd", 0)]
    for s in range(2 * NS):
        so += ([("sd", s + 1)] if s + 1 < 2 * NS else []) + [("so", s)]
    branches = t("ga", 8) + t("lru_out", 8) + t("gc", 8) + t("mem_out", 8)
    return (
        [("mem_sq",)] + t("mk", 8)[:4] + [("x_sq",), ("lam",)] + t("mk", 8)[4:] + weave(t("mv", 8), t("mkT", 4))
        + t("mq", 8) + t("mqs", 2) + weave(t("ux", 8), weave(attn[:11], kl[:2])) + [("conv",)]
        + weave(t("uy", 8), weave(attn[11:], kl[2:5])) + weave(t("q", 8), weave(gates, kl[5:])) + [("rot_q",)]
        + weave(t("k", 8), cache[:5]) + [("rot_k",), ("lru",)] + weave(v[:6], cache[5:]) + [("lru_root",), ("gelu",)]
        + weave(v[6:12], krows) + [("gelu_tanh",)] + v[12:] + [("scT",)]
        + vrows + weave(weave(branches, ret), so) + weave(t("gb", 8), [("soT",)] + t("on", 4)) + t("g", 16)
        + t("ret_out", 8) + t("x2", 8) + [("x2_sq",)]
    )


NO_PSUM = {"lam", "sd", "conv", "kl", "lru", "lru_root", "gelu", "gelu_tanh", "rot_q", "rot_k"}
PROJECTIONS = {"mk", "mv", "mq", "ux", "uy", "q", "k", "v", "g", "ga", "gb", "gc", "lru_out", "ret_out",
               "mem_out", "x2"}


class Steps:

    def __init__(self, engine, default):
        self.engine, self.default, self.count, self.last = engine, default, {}, None

    def did(self, instruction, sem=None):
        sem = self.default if sem is None else sem
        if isinstance(sem, tuple):
            sem, count = sem
        else:
            count = self.count[id(sem)] = self.count.get(id(sem), 0) + 1
        instruction.then_inc(sem, 1)
        self.last = (sem, count)

    def settle(self):
        if self.last:
            self.engine.wait_ge(*self.last)


def build_program(nc, dram, outs, const_at):
    order = tensor_order()
    where, uses, turn = {}, [0] * 8, {"proj": 0, "side": 0}
    for task in order:
        kind = task[0]
        if kind in NO_PSUM:
            continue
        if kind in ("sc", "so"):
            if task[1] == 0:
                uses[7] += 1
            where[task] = (7, uses[7] - 1)
            continue
        if kind in PROJECTIONS:
            bank = turn["proj"] % 4
            turn["proj"] += 1
        else:
            bank = 4 + turn["side"] % 3
            turn["side"] += 1
        where[task] = (bank, uses[bank])
        uses[bank] += 1
    phase1_uses = list(uses)

    def wide(w, col, row=0):
        return w[row:row + D, col:col + 256].rearrange("(k p) n -> p k n", p=P)

    chunks, chunk_of, last_task = [], {}, []

    def chunk(kind, c, ap):
        chunk_of[(kind, c)] = len(chunks)
        chunks.append(ap)
        last_task.append((kind.rstrip("2") if kind == "ret_out2" else kind, 2 * c + 1))

    seen = set()
    for task in order:
        kind = task[0]
        if kind not in PROJECTIONS or task[1] % 2:
            continue
        c = task[1] // 2
        if kind in ("mk", "mv"):
            chunk(kind, c, wide(dram["w_mem_kv"], (0 if kind == "mk" else D) + c * 256))
        elif kind == "lru_out":
            chunk(kind, c, wide(dram["w_branch_lru"], c * 256))
        elif kind == "mem_out":
            chunk(kind, c, wide(dram["w_branch_mem"], c * 256))
        elif kind == "x2":
            chunk(kind, c, wide(dram["w_out"], c * 256))
        elif kind == "ret_out":
            chunk(kind, c, wide(dram["w_branch_ret"], c * 256))
            chunk("ret_out2", c, wide(dram["w_branch_ret"], c * 256, D))
        else:
            chunk(kind, c, wide(dram["w_in"], OFF[kind] + c * 256))
    NCH = len(chunks)
    ring_uses = [len(range(s, NCH, RING1)) if s < RING1 else 0 for s in range(RING)]

    with ExitStack() as ctx:
        place_of = place_buffers()
        arena = ctx.enter_context(nc.sbuf_tensor("arena", [P, ARENA], F32))

        def buf(name):
            at = place_of[name]
            return arena[:, at:at + BUFFERS[name][0]]

        def tiles(ap, n):
            return ap.rearrange("p (k n) -> p k n", k=n)

        ring = arena[:, 0:2 * RING * CHUNK]
        slot = tiles(ring, 2 * RING)
        const = buf("const")

        def k_(name):
            a, b = const_at[name]
            home, first = {"cos": ("rope", 0), "sin": ("rope", 0), "dmask": ("dmask", NROPE)}.get(
                name, ("const", NROPE + NMASK))
            return buf(home)[:, a - first:b - first]

        ident = k_("ident")
        ones = buf("ones")
        chan = buf("chan")
        cv = lambda name, kt: chan[:, CH[name] * KT + kt:CH[name] * KT + kt + 1]
        cvs = lambda name: chan[:, CH[name] * KT:(CH[name] + 1) * KT]
        xT = tiles(buf("xT"), KT)
        x_res = tiles(buf("x"), KT)
        xnT = tiles(buf("xnT"), KT)
        rstd = tiles(buf("rstd"), 2)
        small = buf("small")
        sp4 = buf("sp4")
        brh = buf("brh")
        stats = buf("stats")
        eps_col = buf("eps_col")
        memT = tiles(buf("memT"), KT)
        sq = tiles(buf("sq"), KT)
        wr = tiles(buf("wr"), KT)
        wi = tiles(buf("wi"), KT)
        sconv = buf("sconv").rearrange("p (k j b) -> p k j b", k=KT, j=3)
        slru = tiles(buf("slru"), KT)
        mk_rows = tiles(buf("mk_rows"), 2)
        mv_rows = tiles(buf("mv_rows"), 2)
        mkT = tiles(buf("mkT"), KT)
        mqT = tiles(buf("mqT"), KT)
        mqs_rows = buf("mqs_rows")
        mq_row0 = buf("mq_row0")
        qb = tiles(buf("qb"), 2)
        kv = tiles(buf("kv"), 2)
        prod = buf("prod")
        L = buf("L")
        prob = buf("prob").rearrange("p (a l m) -> p a l m", a=2, l=2)
        probT = tiles(buf("probT"), 2)
        cT = tiles(buf("cT"), KT)
        uxp = tiles(buf("uxp"), KT)
        uc = tiles(buf("uc"), KT)
        convt = buf("convt")
        Tr = tiles(buf("Tr"), KT)
        Ti = tiles(buf("Ti"), KT)
        Rb = tiles(buf("Rb"), KT)
        uyT = tiles(buf("uyT"), KT)
        lru_st = tiles(buf("lru_st"), KT)[:, :, 0:9]
        conv_st = tiles(buf("conv_st"), KT)[:, :, 0:11]
        qT = tiles(buf("qT"), KT)
        kT = tiles(buf("kT"), KT)
        rtmp = buf("rtmp")
        vT = tiles(buf("vT"), VT)
        v_rows = tiles(buf("v_rows"), 2)
        k_rows = tiles(buf("k_rows"), 2)
        vs_rows = buf("vs_rows")
        v_row0 = buf("v_row0")
        vb = tiles(buf("vb"), 2)
        st = buf("st").rearrange("p (s i v) -> p s i v", s=3, i=4)
        p32 = buf("p32")
        PM = buf("PM").rearrange("p (m h b c) -> p m h b c", m=2, h=HEADS, b=NS)
        PMd = place_of["PM"]
        cs = buf("cs")
        QM = buf("QM").rearrange("p (k b c) -> p k b c", k=KT, b=NS)
        QMd = place_of["QM"]
        attT = buf("attT")
        oT = tiles(buf("oT"), VT)
        S_st = tiles(buf("S_st"), 2)
        os_ = buf("os")
        merged = tiles(buf("merged"), KT)
        tgate = tiles(buf("tgate"), KT)
        gt = tiles(buf("gt"), 2)
        sq2 = tiles(buf("sq2"), 4)
        sq3 = tiles(buf("sq3"), KT)
        rout = tiles(buf("rout"), KT)
        rbias = buf("rbias")
        xr = [buf(f"xr{i}").bitcast(BF16).rearrange("p (t d) -> p t d", t=TT) for i in range(3)]
        xres = buf("xres")
        lgt = tiles(buf("lgt"), TT)
        Rc = tiles(buf("Rc"), TT)
        Wc = tiles(buf("Wc"), TT)
        M01 = tiles(buf("M01"), TT)
        tmpA = buf("tmpA")
        tmpB = buf("tmpB")
        tmpC = buf("tmpC")
        tmpD = buf("tmpD")
        ov = buf("ov")
        ints = buf("ints").bitcast(I32)
        eq = tiles(buf("eq"), TT)
        Sw = buf("Sw").rearrange("p (a t s) -> p a t s", a=2, t=TT)
        Sb = buf("Sb").bitcast(BF16).rearrange("p (a t s) -> p a t s", a=2, t=TT)
        XgT = buf("XgT").rearrange("p (a k s) -> p a k s", a=2, k=KT)
        SwT = tiles(buf("SwT"), 2)
        tg = buf("tg")
        hid = buf("hid")
        hT = buf("hT").rearrange("p (j a s) -> p j a s", j=2, a=2)
        yS = tiles(buf("yS"), 2)
        acc = tiles(buf("acc"), KT)
        tmid = buf("tmid")
        zero_row = buf("zero_row")
        hid_z = buf("hid_z")

        def diagonal(at, n):
            return arena[:, at:at + 64 * n].rearrange("p (k x) -> p k x", x=64)[:, :, 0:64:9]

        psum = ctx.enter_context(nc.psum_tensor("psum", [P, 8, 512], F32))

        sem = lambda name: ctx.enter_context(nc.semaphore(name))
        psum_full = [sem(f"psum_full_{b}") for b in range(8)]
        psum_free = [sem(f"psum_free_{b}") for b in range(8)]
        chunk_loaded = [sem(f"chunk_loaded_{s}") for s in range(2 * RING)]
        x_again = sem("x_again")
        mem_in, x_in, const_in, gate_in = sem("mem_in"), sem("x_in"), sem("const_in"), sem("gate_in")
        act_step, dve_step = sem("act_step"), sem("dve_step")
        pool_step = sem("pool_step")
        ones_set = sem("ones_set")
        squares = sem("squares")
        root = sem("root")
        mem_normed, x_normed = sem("mem_normed"), sem("x_normed")
        neg_max = sem("neg_max")
        prob_normed = sem("prob_normed")
        q_row_in, q_bcast = sem("q_row_in"), sem("q_bcast")
        kv_in = [sem("kv_in_0"), sem("kv_in_1")]
        k_used, v_used = sem("k_used"), sem("v_used")
        probs_spread, bank7_zero = sem("probs_spread"), sem("bank7_zero")
        cache_neg_max, pads_zero = sem("cache_neg_max"), sem("pads_zero")
        x3_ready, eq_built, swish_mid = sem("x3_ready"), sem("eq_built"), sem("swish_mid")
        lam_abs, lam_exp, rates = sem("lam_abs"), sem("lam_exp"), sem("rates")
        conv_done, gate_act, lru_roots_in, lru_roots = sem("conv_done"), sem("gate_act"), sem("lru_roots_in"), sem("lru_roots")
        gelu_in, gelu_tanh, lru_ready = sem("gelu_in"), sem("gelu_tanh"), sem("lru_ready")
        q_rotated, k_rotated = sem("q_rotated"), sem("k_rotated")
        v_row_in, v_bcast = sem("v_row_in"), sem("v_bcast")
        st_in = [sem(f"st_in_{i}") for i in range(3)]
        st_out = [sem(f"st_out_{i}") for i in range(3)]
        st_decayed, st_updated, st_read = sem("st_decayed"), sem("st_updated"), sem("st_read")
        att_masked = sem("att_masked")
        s_out = [sem("s_out_0"), sem("s_out_1")]
        o_normed, g_tanh, ret_ready = sem("o_normed"), sem("g_tanh"), sem("ret_ready")
        branch_merged = sem("branch_merged")
        stored = sem("stored")
        lru_staged, conv_staged = sem("lru_staged"), sem("conv_staged")
        x2_normed, x_split, routed_masks = sem("x2_normed"), sem("x_split"), sem("routed_masks")
        row_high, row_rest, row_mid = sem("row_high"), sem("row_rest"), sem("row_mid")
        router_exp_in, router_exp = sem("router_exp_in"), sem("router_exp")
        routed = sem("routed")
        scratch_dead = sem("scratch_dead")
        onehot_built, gather_full, scatterT_full = sem("onehot_built"), sem("gather_full"), sem("scatterT_full")
        tokens_ready, scatterT_ready = sem("tokens_ready"), sem("scatterT_ready")
        gate_up_full, gate_tanh, hid_ready = sem("gate_up_full"), sem("gate_tanh"), sem("hid_ready")
        hidT_full, hidT_ready = sem("hidT_full"), sem("hidT_ready")
        y_full, y_ready = sem("y_full"), sem("y_ready")
        scatter_full, scatter_added = sem("scatter_full"), sem("scatter_added")
        tiles03_used, down01_used = sem("tiles03_used"), sem("down01_used")
        pool_out = sem("pool_out")
        final_normed, final_sum, final_root = sem("final_normed"), sem("final_sum"), sem("final_root")
        row_full, logits_full, masks_ready, ranks_full = sem("row_full"), sem("logits_full"), sem("masks_ready"), sem("ranks_full")

        def states_stored(eng):
            for i in range(3):
                eng.wait_ge(st_out[i], 16 * len(range(i, 2 * NS, 3)))
            for i in range(2):
                eng.wait_ge(s_out[i], 16 * HEADS)

        def full(eng, task):
            b, n = where[task]
            eng.wait_ge(psum_full[b], n + 1)

        def read(eng, task):
            b, n = where[task]
            eng.wait_ge(psum_free[b], n + 1)

        def ps(task):
            return psum[:, where[task][0], :]

        def free_of(task):
            b, n = where[task]
            return psum_free[b], n + 1

        XSQ = {"mem_sq": 1, "x_sq": 2}
        last = {k: (k, n - 1) for k, n in (("mk", 8), ("mv", 8), ("mq", 8), ("ux", 8), ("uy", 8), ("q", 8), ("k", 8),
                                            ("v", 16), ("ga", 8), ("gb", 8), ("gc", 8))}
        n_state = lambda s: (s // 2, s % 2)


        def router_products(pe):
            pe.wait_ge(x2_normed, 1)
            for t in range(TT):
                n = min(P, T - t * P)
                for k4 in range(2):
                    u = 2 * t + k4
                    if u >= 2:
                        pe.wait_ge(row_rest, u - 1)
                    for k in range(4):
                        mm = pe.transpose(psum[0:n, u % 2, k * P:(k + 1) * P], xnT[:, 4 * k4 + k, t * P:t * P + n],
                                          ident)
                    mm.then_inc(row_full, 1)
                for k in range(KT):
                    pe.matmul(psum[0:n, 2, t * 64:t * 64 + NLOG], xnT[:, k, t * P:t * P + n], rout[:, k, :],
                              start=k == 0, stop=False)
                mm = pe.matmul(psum[0:n, 2, t * 64:t * 64 + NLOG], ones[0:1, 0:n], rbias[0:1, 0:NLOG],
                               start=False, stop=True)
            mm.then_inc(logits_full, 1)
            pe.wait_ge(masks_ready, 1)
            for t in range(TT):
                for s in range(t):
                    pe.matmul(psum[:, 3, t * 64:t * 64 + EXPERTS], ones, M01[:, s, :], start=s == 0, stop=False)
                pe.matmul(psum[:, 3, t * 64:t * 64 + EXPERTS], k_("before"), M01[:, t, :], start=t == 0, stop=True)
            for s in range(TT):
                mm = pe.matmul(psum[:, 3, 192:192 + EXPERTS], ones, M01[:, s, :], start=s == 0, stop=s == TT - 1)
            mm.then_inc(ranks_full, 1)

        def gather(pe, g, half, built=1):
            pe.wait_ge(onehot_built, g + built)
            if not isinstance(g, int):
                pe.wait_ge(tokens_ready, g)
            for k in range(KT):
                for t in range(TT):
                    for x in range(3):
                        mm = pe.matmul(psum[:, 0, k * SLOTS:(k + 1) * SLOTS], xr[x][:, t, k * P:(k + 1) * P],
                                       Sb[:, half, t, :], start=t == 0 and x == 0, stop=t == TT - 1 and x == 2)
            mm.then_inc(gather_full, 1)
            if not isinstance(g, int):
                pe.wait_ge(scatterT_ready, g + 1)
            for t in range(TT):
                n = min(P, T - t * P)
                mm = pe.transpose(psum[:, 1, t * P:t * P + n], Sw[0:n, half, t, :], ident[0:n, 0:n])
            mm.then_inc(scatterT_full, 1)

        def gate_up(pe, e, g, half, lag):
            base = RING if half == 0 else 0
            pe.wait_ge(tokens_ready, g + 1)
            pe.wait_ge(hid_ready, e + 1)
            for k in range(KT):
                s = base + 2 * (k // 4)
                if k % 4 == 0:
                    for i in range(2):
                        expert_loaded(pe, e, s + i, half, lag)
                w = slot[:, s:s + 2, :].rearrange("p a (k n) -> p a k n", k=4)[:, :, k % 4, :]
                for a in range(2):
                    mm = pe.matmul(psum[64 * a:64 * a + SLOTS, 2, :], XgT[:, half, k, :],
                                   w[:, :, 256 * a:256 * a + 256], start=k == 0, stop=k == KT - 1)
                if k == 3:
                    mm.then_inc(tiles03_used, 1)
            mm.then_inc(gate_up_full, 1)

        def expert_loaded(pe, e, s, half, lag):
            first = 0 if s >= RING else 16 * ring_uses[s]
            if lag == 2:
                pe.wait_ge(chunk_loaded[s], 8 * e + (first + 16 - 8 * half))
            else:
                pe.wait_ge(chunk_loaded[s], 16 * e + (16 + 16 * (EXPERTS // 2) - 16 * EXPERTS))

        def hidden_T(pe, e):
            pe.wait_ge(hid_ready, e + 2)
            pe.wait_ge(hidT_ready, e + 1)
            for j in range(2):
                mm = pe.transpose(psum[:, 3, j * P:(j + 1) * P], hid[:, j * P:(j + 1) * P], ident)
            mm.then_inc(hidT_full, 1)

        def down(pe, e, half, lag):
            base = RING if half == 0 else 0
            pe.wait_ge(hidT_ready, e + 2)
            pe.wait_ge(y_ready, e + 1)
            for i in range(2):
                expert_loaded(pe, e, base + 4 + i, half, lag)
                w = slot[:, base + 4 + i, :].rearrange("p (k n) -> p k n", k=2)
                for dh in range(2):
                    for a in range(2):
                        mm = pe.matmul(psum[64 * a:64 * a + SLOTS, 4 + dh, :], hT[:, a, i, :],
                                       w[:, a, dh * 512:(dh + 1) * 512], start=i == 0, stop=i == 1)
                if i == 0:
                    mm.then_inc(down01_used, 1)
            mm.then_inc(y_full, 1)

        def scatter(pe, n, g, half):
            pe.wait_ge(y_ready, n + 1)
            pe.wait_ge(scatterT_ready, g)
            for d in range(KT):
                pe.wait_ge(scatter_added, n * KT + (d + 1))
                pe.matmul(psum[:, 6 + d % 2, 0:T], yS[:, half, d * P:(d + 1) * P], SwT[:, half, :],
                          start=True, stop=True).then_inc(scatter_full, 1)

        block = ctx.enter_context(nc.Block())

        @block.sync
        def _(sp):
            sp.dma_start(const, dram["const"][:, NROPE + NMASK:]).then_inc(const_in, 16)
            sp.dma_start(chan, dram["chan"]).then_inc(const_in, 16)
            for h in range(2):
                sp.dma_start(memT[:, 4 * h:4 * h + 4], dram["memT"].rearrange("(k p) n -> p k n", p=P)[:, 4 * h:4 * h + 4]).then_inc(mem_in, 16)
            sp.dma_start(slot[:, 0, :].rearrange("p (k n) -> p k n", k=KT), chunks[0]).then_inc(chunk_loaded[0], 16)
            sp.dma_start(xT[:], dram["xT"].rearrange("(k p) n -> p k n", p=P)).then_inc(x_in, 16)
            for n in range(1, NCH):
                if n == 4:
                    sp.dma_start(wr, dram["w_r"].rearrange("n c d -> c n d")).then_inc(gate_in, 16)
                    sp.dma_start(wi, dram["w_i"].rearrange("n c d -> c n d")).then_inc(gate_in, 16)
                    sp.dma_start(sconv, dram["sconv"].rearrange("p (k j b) -> p k j b", k=KT, j=3)).then_inc(gate_in, 16)
                    sp.dma_start(slru, dram["slru"].rearrange("p (k b) -> p k b", k=KT)).then_inc(gate_in, 16)
                    sp.dma_start(rout, dram["router"].rearrange("(k p) n -> p k n", p=P)).then_inc(gate_in, 16)
                    sp.dma_start(rbias[0:1, :NLOG], dram["rbias"]).then_inc(gate_in, 16)
                    sp.dma_start(buf("rope"), dram["const"][:, 0:NROPE]).then_inc(gate_in, 16)
                    sp.dma_start(buf("dmask"), dram["const"][:, NROPE:NROPE + NMASK]).then_inc(gate_in, 16)
                if n == chunk_of[("g", 0)]:
                    states_stored(sp)
                    sp.dma_start(x_res[:], dram["xT"].rearrange("(k p) n -> p k n", p=P)).then_inc(x_again, 16)
                if n >= RING1:
                    full(sp, last_task[n - RING1])
                sp.dma_start(slot[:, n % RING1, :].rearrange("p (k n) -> p k n", k=KT), chunks[n]).then_inc(
                    chunk_loaded[n % RING1], 16)

            wg = dram["w_gate"].rearrange("g e (k p) f -> (g e) p k f", p=P)
            wu = dram["w_up"].rearrange("g e (k p) f -> (g e) p k f", p=P)
            wd = dram["w_down"].rearrange("g e (k p) d -> (g e) p k d", p=P)

            def expert_part(e, i):
                w = (wg, wu, wg, wu, wd, wd)[i]
                if i < 4:
                    lo = 4 * (i // 2)
                    return w[bass.ds(e, 1), :, lo:lo + 4, :].rearrange("a p k f -> p (a k) f")
                lo = 2 * (i - 4)
                return w[bass.ds(e, 1), :, lo:lo + 2, :].rearrange("a p k f -> p (a k) f")

            def into(s, i):
                return slot[:, s, :].rearrange("p (k n) -> p k n", k=4 if i < 4 else 2)

            sp.wait_ge(ret_ready, VT)
            states_stored(sp)
            for i in range(6):
                sp.dma_start(into(RING + i, i), expert_part(0, i)).then_inc(chunk_loaded[RING + i], 16)
            for i in range(6):
                if i < RING1:
                    full(sp, last_task[max(n for n in range(NCH) if n % RING1 == i)])
                sp.dma_start(into(i, i), expert_part(1, i)).then_inc(chunk_loaded[i], 16)
            part_used = (tiles03_used, tiles03_used, gate_up_full, gate_up_full, down01_used, y_full)
            with sp.Fori(1, EXPERTS // 2) as pair:
                for j in range(2):
                    e = sp.snap(pair * 2 + j)
                    base = RING if j == 0 else 0
                    for i in range(6):
                        sp.wait_ge(part_used[i], e - 1)
                        sp.dma_start(into(base + i, i), expert_part(e, i)).then_inc(chunk_loaded[base + i], 16)
            sp.wait_ge(routed, 1)
            n_over = sp.value_load(ints[0:1, 0:1], min_val=0, max_val=OVER)
            with sp.If(n_over > 0):
                with sp.Fori(0, n_over) as j:
                    e = sp.value_load(ints[0:1, bass.ds(j + 8, 1)], min_val=0, max_val=EXPERTS - 1)
                    for i in range(6):
                        sp.wait_ge(part_used[i], j + EXPERTS)
                        sp.dma_start(into(RING + i, i), expert_part(e, i)).then_inc(chunk_loaded[RING + i], 16)
            with sp.Else():
                sp.nop()
            sp.nop()
            for q in range(4):
                sp.wait_ge(final_normed, 2 * q + 2)
                sp.dma_start(outs["y"].rearrange("(k p) n -> p k n", p=P)[:, 2 * q:2 * q + 2],
                             acc[:, 2 * q:2 * q + 2]).then_inc(stored, 16)
            sp.wait_ge(stored, 16 * 4)
            sp.nop()

        @block.gpsimd
        def _(pool):
            n_stored = 0
            sc_src = dram["state_conv"][:, 1:3, :]
            pool.dma_start(outs["conv_keep"], sc_src).then_inc(pool_out, 16)
            n_stored += 1

            def load_kv(n):
                b = n % NS
                src = dram["cache_mem_k" if n < NS else "cache_mem_v"][b].rearrange("(m p) h d -> p m (h d)", p=P)
                pool.dma_start(kv[:, n % 2, :].rearrange("p (m d) -> p m d", m=2), src).then_inc(kv_in[n % 2], 16)

            def q_broadcast(b):
                if b >= 1:
                    pool.wait_ge(q_bcast, b)
                pool.dma_start(mq_row0[0:1, :], mqs_rows[b:b + 1, :]).then_inc(q_row_in, 16)
                pool.wait_ge(q_row_in, 16 * (b + 1))
                if b >= 2:
                    pool.wait_ge(k_used, b - 1)
                nc.gpsimd.partition_broadcast(qb[:, b % 2, :], mq_row0[0:1, :], P).then_inc(q_bcast, 1)

            read(pool, last["mk"])
            pool.dma_start(outs["mem_k"].rearrange("(m p) d -> p m d", p=P), mk_rows).then_inc(pool_out, 16)
            read(pool, last["mv"])
            pool.dma_start(outs["mem_v"].rearrange("(m p) d -> p m d", p=P), mv_rows).then_inc(pool_out, 16)
            n_stored += 2
            pool.wait_ge(x_normed, 1)
            load_kv(0)
            load_kv(1)
            read(pool, ("mqs", 1))
            for b in range(NS):
                q_broadcast(b)
                if b >= 1:
                    pool.wait_ge(k_used, b)
                    load_kv(b + 1)
            pool.wait_ge(k_used, NS)
            load_kv(NS + 1)
            for b in range(2, NS):
                pool.wait_ge(v_used, b - 1)
                load_kv(NS + b)
                if b == 3:
                    pool.wait_ge(conv_staged, 1)
                    pool.dma_start(outs["conv_new"], conv_st).then_inc(pool_out, 16)
                    n_stored += 1
            pool.wait_ge(lru_staged, 1)
            pool.dma_start(outs["lru"], lru_st).then_inc(pool_out, 16)
            n_stored += 1

            def load_state(s):
                b, hp = n_state(s)
                src = dram["state_ret"][b, 2 * hp:2 * hp + 2].rearrange("h (i p) v -> p (h i) v", p=P)
                if s >= 3:
                    pool.wait_ge(st_out[s % 3], 16 * (s // 3))
                    pool.wait_ge(st_read, s - 2)
                pool.dma_start(st[:, s % 3], src).then_inc(st_in[s % 3], 16)

            def v_broadcast(s):
                b, hp = n_state(s)
                if s >= 1:
                    pool.wait_ge(v_bcast, s)
                pool.dma_start(v_row0[0:1, :], vs_rows[b:b + 1, hp * D:(hp + 1) * D]).then_inc(v_row_in, 16)
                pool.wait_ge(v_row_in, 16 * (s + 1))
                if s >= 2:
                    pool.wait_ge(st_updated, s - 1)
                nc.gpsimd.partition_broadcast(vb[:, s % 2, :], v_row0[0:1, :], P).then_inc(v_bcast, 1)

            read(pool, ("vs", 3))
            read(pool, ("scT",))
            pool.wait_ge(lru_ready, 1)
            load_state(0)
            load_state(1)
            load_state(2)
            v_broadcast(0)
            v_broadcast(1)
            for s in range(2 * NS):
                b, hp = n_state(s)
                pool.wait_ge(st_updated, s + 1)
                dst = outs["ret_s"][b, 2 * hp:2 * hp + 2].rearrange("h (i p) v -> p (h i) v", p=P)
                pool.dma_start(dst, st[:, s % 3]).then_inc(st_out[s % 3], 16)
                if s + 2 < 2 * NS:
                    v_broadcast(s + 2)
                    if s >= 1:
                        load_state(s + 2)
            states_stored(pool)
            pool.wait_ge(pool_out, 16 * n_stored)
            nc.gpsimd.nop()

        @block.tensor
        def _(pe):
            def begin(task):
                b, n = where[task]
                if n >= 1:
                    pe.wait_ge(psum_free[b], n)

            def end(task, mm):
                mm.then_inc(psum_full[where[task][0]], 1)

            def loaded(n):
                pe.wait_ge(chunk_loaded[n % RING1], 16 * (n // RING1 + 1))

            def weights(n):
                return slot[:, n % RING1, :].rearrange("p (k n) -> p k n", k=KT)

            def project(task, rhs):
                kind, i = task
                n = chunk_of[(kind, i // 2)]
                loaded(n)
                begin(task)
                w = weights(n)
                two = kind == "ret_out"
                for k in range(KT):
                    mm = pe.matmul(ps(task)[:, 0:T], w[:, k, (i % 2) * P:(i % 2 + 1) * P], rhs[:, k, :],
                                   start=k == 0, stop=k == KT - 1 and not two)
                if two:
                    n += 1
                    loaded(n)
                    w = weights(n)
                    for k in range(KT):
                        mm = pe.matmul(ps(task)[:, 0:T], w[:, k, (i % 2) * P:(i % 2 + 1) * P], rhs[:, KT + k, :],
                                       start=False, stop=k == KT - 1)
                end(task, mm)

            def column_sums(task, src, n, cols):
                begin(task)
                for k in range(n):
                    mm = pe.matmul(ps(task)[:, 0:cols], ones, src[:, k, 0:cols], start=k == 0, stop=k == n - 1)
                end(task, mm)

            rhs_of = {"mq": xnT, "ux": xnT, "uy": xnT, "q": xnT, "k": xnT, "v": xnT, "g": xnT, "ga": xnT,
                      "gb": xnT, "gc": xnT, "lru_out": uyT, "ret_out": oT, "mem_out": cT, "x2": merged}
            pe.wait_ge(const_in, 32)
            pe.wait_ge(ones_set, 1)
            for task in order:
                kind = task[0]
                if kind in NO_PSUM:
                    continue
                if kind == "mem_sq":
                    pe.wait_ge(squares, 1)
                    column_sums(task, sq, KT, TP)
                elif kind == "x_sq":
                    pe.wait_ge(squares, 2)
                    column_sums(task, sq, KT, T)
                elif kind in ("mk", "mv"):
                    i = task[1]
                    n = chunk_of[(kind, i // 2)]
                    if task == ("mk", 0):
                        pe.wait_ge(mem_normed, 1)
                    loaded(n)
                    begin(task)
                    w = weights(n)
                    m = i % 2
                    for k in range(KT):
                        mm = pe.matmul(ps(task)[:, 0:256], memT[:, k, m * P:(m + 1) * P], w[:, k, :],
                                       start=k == 0, stop=k == KT - 1)
                    end(task, mm)
                elif kind in rhs_of:
                    if task == ("mq", 0):
                        pe.wait_ge(x_normed, 1)
                    if task == ("lru_out", 0):
                        pe.wait_ge(lru_ready, 1)
                    if task == ("ret_out", 0):
                        pe.wait_ge(ret_ready, VT)
                    if task == ("mem_out", 0):
                        read(pe, ("pv", 3, 1))
                        read(pe, ("scT",))
                    if task == ("x2", 0):
                        pe.wait_ge(branch_merged, 2 * KT)
                    project(task, rhs_of[kind])
                elif kind == "mkT":
                    q = task[1]
                    read(pe, last["mk"])
                    begin(task)
                    for k in range(2):
                        for m in range(2):
                            mm = pe.transpose(ps(task)[:, (2 * k + m) * P:(2 * k + m + 1) * P],
                                              mk_rows[:, m, (2 * q + k) * P:(2 * q + k + 1) * P], ident)
                    end(task, mm)
                elif kind == "mqs":
                    read(pe, last["mq"])
                    begin(task)
                    for k in range(4):
                        mm = pe.transpose(ps(task)[0:NS, k * P:(k + 1) * P], mqT[:, 4 * task[1] + k, TP:T], ident)
                    end(task, mm)
                elif kind == "lg":
                    _, h, l = task
                    read(pe, ("mkT", 3))
                    read(pe, last["mq"])
                    begin(task)
                    for i in range(2):
                        mm = pe.matmul(ps(task)[:, 0:TP], mqT[:, 2 * h + i, l * P:(l + 1) * P], mkT[:, 2 * h + i, :],
                                       start=i == 0, stop=i == 1)
                    end(task, mm)
                elif kind == "pT":
                    h = task[1]
                    pe.wait_ge(prob_normed, 2 * h + 2)
                    begin(task)
                    for m in range(2):
                        for l in range(2):
                            mm = pe.transpose(ps(task)[:, (2 * m + l) * P:(2 * m + l + 1) * P],
                                              prob[:, h % 2, l, m * P:(m + 1) * P], ident)
                    end(task, mm)
                elif kind == "pv":
                    _, h, j = task
                    read(pe, ("pT", h))
                    begin(task)
                    for m in range(2):
                        mm = pe.matmul(ps(task)[:, 0:TP], mv_rows[:, m, (2 * h + j) * P:(2 * h + j + 1) * P],
                                       probT[:, m, :], start=m == 0, stop=m == 1)
                    end(task, mm)
                elif kind in ("r", "i"):
                    n = task[1]
                    pe.wait_ge(conv_done, 1)
                    pe.wait_ge(gate_in, 16 * 8)
                    begin(task)
                    end(task, pe.matmul(ps(task)[:, 0:T], (wr if kind == "r" else wi)[:, n, :], uc[:, n, :],
                                        start=True, stop=True))
                elif kind == "kr":
                    _, m, q = task
                    pe.wait_ge(k_rotated, 1)
                    begin(task)
                    for k in range(4):
                        mm = pe.transpose(ps(task)[:, k * P:(k + 1) * P], kT[:, 4 * q + k, m * P:(m + 1) * P], ident)
                    end(task, mm)
                elif kind == "sl":
                    pe.wait_ge(k_used, NS)
                    begin(task)
                    for m in range(2):
                        mm = pe.transpose(ps(task)[0:32, m * P:(m + 1) * P], L[:, 32 * m:32 * m + 32], ident)
                    end(task, mm)
                elif kind == "spT":
                    pe.wait_ge(prob_normed, 2 * HEADS + 1)
                    begin(task)
                    for m in range(2):
                        mm = pe.transpose(ps(task)[:, m * 32:m * 32 + 32], p32[0:32, m * P:(m + 1) * P],
                                          ident[0:32, 0:32])
                    end(task, mm)
                elif kind == "sc":
                    b = task[1]
                    if b == 0:
                        read(pe, ("spT",))
                        pe.wait_ge(bank7_zero, 1)
                    n = NS + b
                    pe.wait_ge(kv_in[n % 2], 16 * (n // 2 + 1))
                    for m in range(2):
                        for h in range(HEADS):
                            mm = pe.matmul(psum[32 * h:32 * h + NS, 7, 0:DK], PM[:, m, h, b, :],
                                           kv[:, n % 2, m * D + h * DK:m * D + (h + 1) * DK],
                                           start=b == 0 and m == 0, stop=b == NS - 1 and m == 1)
                    mm.then_inc(v_used, 1)
                elif kind == "scT":
                    read(pe, ("sc", NS - 1))
                    begin(task)
                    for j in range(2):
                        mm = pe.transpose(ps(task)[:, j * P:(j + 1) * P], cs[:, j * P:(j + 1) * P], ident)
                    end(task, mm)
                elif kind == "vs":
                    read(pe, last["v"])
                    begin(task)
                    for k in range(4):
                        mm = pe.transpose(ps(task)[0:NS, k * P:(k + 1) * P], vT[:, 4 * task[1] + k, TP:T], ident)
                    end(task, mm)
                elif kind == "vr":
                    _, m, q = task
                    begin(task)
                    for k in range(4):
                        mm = pe.transpose(ps(task)[:, k * P:(k + 1) * P], vT[:, 4 * q + k, m * P:(m + 1) * P], ident)
                    end(task, mm)
                elif kind == "att":
                    h = task[1]
                    pe.wait_ge(q_rotated, 1)
                    begin(task)
                    for i in range(2):
                        pe.matmul(ps(task)[:, 0:TP], kT[:, 2 * h + i, 0:P], qT[:, 2 * h + i, 0:TP],
                                  start=i == 0, stop=i == 1)
                    for i in range(2):
                        mm = pe.matmul(ps(task)[:, TP:TP + P], kT[:, 2 * h + i, P:TP], qT[:, 2 * h + i, P:TP],
                                       start=i == 0, stop=i == 1)
                    end(task, mm)
                elif kind == "o":
                    _, h, j = task
                    if j == 0:
                        read(pe, ("att", h))
                        read(pe, ("vr", 1, 3))
                    begin(task)
                    c = h * DV + j * P
                    pe.matmul(ps(task)[:, 0:TP], v_rows[:, 0, c:c + P], attT[:, 0:TP], start=True, stop=False)
                    end(task, pe.matmul(ps(task)[:, P:TP], v_rows[:, 1, c:c + P], attT[:, TP:TP + P],
                                        start=False, stop=True))
                elif kind == "S":
                    _, h, i = task
                    if i == 0:
                        read(pe, ("kr", 1, 1))
                    begin(task)
                    for m in range(2):
                        mm = pe.matmul(ps(task)[:, 0:DV], k_rows[:, m, (2 * h + i) * P:(2 * h + i + 1) * P],
                                       v_rows[:, m, h * DV:(h + 1) * DV], start=m == 0, stop=m == 1)
                    end(task, mm)
                elif kind == "so":
                    s = task[1]
                    b, hp = n_state(s)
                    if s == 0:
                        pe.wait_ge(bank7_zero, 2)
                    pe.wait_ge(st_updated, s + 1)
                    for i in range(2):
                        for h2 in range(2):
                            h = 2 * hp + h2
                            mm = pe.matmul(psum[32 * h:32 * h + NS, 7, :], QM[:, 2 * h + i, b, :],
                                           st[:, s % 3, 2 * h2 + i, :],
                                           start=b == 0 and i == 0, stop=b == NS - 1 and i == 1)
                    mm.then_inc(st_read, 1)
                elif kind == "soT":
                    read(pe, ("so", 0))
                    begin(task)
                    for j in range(4):
                        mm = pe.transpose(ps(task)[:, j * P:(j + 1) * P], os_[:, j * P:(j + 1) * P], ident)
                    end(task, mm)
                elif kind == "on":
                    pe.wait_ge(squares, 3 + task[1])
                    column_sums(task, sq2, 4, T)
                elif kind == "x2_sq":
                    pe.wait_ge(squares, 3 + HEADS)
                    column_sums(task, sq3, KT, T)
                else:
                    raise AssertionError(kind)

            router_products(pe)
            gather(pe, 0, 0)
            with pe.Fori(0, EXPERTS, 2) as e0:
                for j in range(2):
                    gate_up(pe, e0 + j, e0 + j, j, 2)
                    scatter(pe, e0 + j, e0 + (j + 1), 1 - j)
                    hidden_T(pe, e0 + j)
                    gather(pe, e0 + (j + 1), 1 - j)
                    down(pe, e0 + j, j, 2)
            scatter(pe, EXPERTS, EXPERTS + 1, 1)
            n_over = pe.value_load(ints[0:1, 0:1], min_val=0, max_val=OVER)
            with pe.If(n_over > 0):
                with pe.Fori(0, n_over) as j:
                    gather(pe, j + (EXPERTS + 1), 0, 2)
                    gate_up(pe, j + EXPERTS, j + (EXPERTS + 1), 0, 1)
                    hidden_T(pe, j + EXPERTS)
                    down(pe, j + EXPERTS, 0, 1)
                    scatter(pe, j + (EXPERTS + 1), j + (EXPERTS + 3), 0)
            with pe.Else():
                pe.nop()
            pe.nop()
            pe.wait_ge(squares, 4 + HEADS)
            for k in range(KT):
                mm = pe.matmul(psum[:, 0, 0:T], ones, sq3[:, k, :], start=k == 0, stop=k == KT - 1)
            mm.then_inc(final_sum, 1)

        @block.scalar
        def _(act):
            steps = Steps(act, act_step)

            def run(out, in_, func, sem=None, **kw):
                steps.did(nc.scalar.activation(out, in_, func, **kw), sem)

            def norm_root(task, cols, slot_, width):
                full(act, task)
                run(rstd[:, slot_, 0:cols], ps(task)[:, 0:cols], ACT.Sqrt, free_of(task), scale=1.0 / width,
                    bias=eps_col[:, 0:1])

            act.wait_ge(ones_set, 2)
            act.wait_ge(mem_in, 32)
            for task in order:
                kind = task[0]
                if kind == "mem_sq":
                    run(sq[:, :, 0:TP], memT, ACT.Square, squares)
                    norm_root(task, TP, 0, D)
                elif kind == "x_sq":
                    act.wait_ge(x_in, 16)
                    run(sq, xT, ACT.Square, squares)
                    norm_root(task, T, 1, D)
                elif kind == "lam":
                    act.wait_ge(lam_abs, 1)
                    run(small[:, 0:KT], small[:, 0:KT], ACT.Exp, lam_exp, scale=-1.0)
                elif kind in ("mk", "mv"):
                    i = task[1]
                    full(act, task)
                    dst = mk_rows if kind == "mk" else mv_rows
                    run(dst[:, i % 2, (i // 2) * 256:(i // 2 + 1) * 256], ps(task)[:, 0:256], ACT.Copy, free_of(task))
                elif kind in ("mq", "uy", "q", "v", "ux"):
                    i = task[1]
                    full(act, task)
                    if task == ("ux", 0):
                        act.wait_ge(pads_zero, 1)
                        act.wait_ge(pool_out, 16 * 3)
                    dst = {"mq": mqT, "uy": uyT, "q": qT, "v": vT, "ux": uxp}[kind]
                    lo = 3 if kind == "ux" else 0
                    run(dst[:, i, lo:lo + T], ps(task)[:, 0:T], ACT.Copy, free_of(task))
                elif kind == "k":
                    full(act, task)
                    run(kT[:, task[1], :], ps(task)[:, 0:T], ACT.Copy, free_of(task), scale=DK ** -0.5)
                elif kind == "mkT":
                    q = task[1]
                    full(act, task)
                    run(mkT[:, 2 * q:2 * q + 2, :], ps(task).rearrange("p (k n) -> p k n", k=2), ACT.Copy, free_of(task))
                elif kind == "mqs":
                    full(act, task)
                    run(mqs_rows[0:NS, 512 * task[1]:512 * task[1] + 512], ps(task)[0:NS, :], ACT.Copy, free_of(task))
                elif kind == "lg":
                    _, h, l = task
                    act.wait_ge(neg_max, 2 * h + l + 1)
                    if h >= 2:
                        full(act, ("pT", h - 2))
                    run(prob[:, h % 2, l, :], ps(task)[:, 0:TP], ACT.Exp, free_of(task), scale=DK ** -0.5,
                        bias=stats[:, 2 * h + l:2 * h + l + 1], accum_out=stats[:, 8 + 2 * h + l:9 + 2 * h + l])
                elif kind == "pT":
                    h = task[1]
                    full(act, task)
                    if h >= 1:
                        full(act, ("pv", h - 1, 1))
                    run(probT, ps(task).rearrange("p (m l) -> p m l", m=2), ACT.Copy, free_of(task))
                elif kind == "pv":
                    _, h, j = task
                    full(act, task)
                    run(cT[:, 2 * h + j, 0:TP], ps(task)[:, 0:TP], ACT.Copy, free_of(task))
                elif kind in ("r", "i"):
                    n = task[1]
                    full(act, task)
                    act.wait_ge(rates, 1)
                    dst = (Tr if kind == "r" else Ti)[:, n, :]
                    col = n if kind == "r" else KT + n
                    run(dst, ps(task)[:, 0:T], ACT.Tanh, free_of(task), scale=0.5, bias=brh[:, col:col + 1])
                    if kind == "r":
                        steps.settle()
                        run(dst, dst, ACT.Tanh, scale=sp4[:, n:n + 1], bias=sp4[:, n:n + 1])
                elif kind == "lru_root":
                    act.wait_ge(lru_roots_in, 1)
                    run(Rb, Rb, ACT.Sqrt, lru_roots, scale=2.0, bias=eps_col[:, 1:2])
                    run(Tr, Tr, ACT.Sqrt, lru_roots)
                elif kind == "gelu_tanh":
                    act.wait_ge(gelu_in, 1)
                    run(Ti, Ti, ACT.Tanh, gelu_tanh, scale=float(np.sqrt(2.0 / np.pi)))
                elif kind == "kr":
                    _, m, q = task
                    full(act, task)
                    for h2 in range(2):
                        h = 2 * q + h2
                        c = HEADS * m + h
                        run(k_rows[:, m, 256 * h:256 * h + 256], ps(task)[:, 256 * h2:256 * h2 + 256], ACT.Copy,
                            free_of(task) if h2 else None, scale=k_("kdec")[:, c:c + 1])
                elif kind == "sl":
                    act.wait_ge(cache_neg_max, 1)
                    run(p32[0:32, :], ps(task)[0:32, 0:TP], ACT.Exp, free_of(task), scale=DK ** -0.5,
                        bias=stats[0:32, 16:17], accum_out=stats[0:32, 17:18])
                elif kind == "sc" and task[1] == NS - 1:
                    act.wait_ge(v_used, NS)
                    run(cs, psum[:, 7, 0:TP], ACT.Copy, psum_free[7])
                elif kind == "vs":
                    full(act, task)
                    q = task[1]
                    run(vs_rows[0:NS, 512 * q:512 * q + 512], ps(task)[0:NS, :], ACT.Copy, free_of(task))
                elif kind == "vr":
                    _, m, q = task
                    full(act, task)
                    run(v_rows[:, m, 512 * q:512 * q + 512], ps(task), ACT.Copy, free_of(task))
                elif kind in ("ga", "gb", "gc"):
                    i = task[1]
                    full(act, task)
                    if kind == "gb":
                        act.wait_ge(branch_merged, i + 1)
                    run((merged if kind == "ga" else tgate)[:, i, :], ps(task)[:, 0:T], ACT.Tanh, free_of(task), scale=0.5)
                elif kind == "sd":
                    s = task[1]
                    b, hp = n_state(s)
                    act.wait_ge(st_in[s % 3], 16 * (s // 3 + 1))
                    for h2 in range(2):
                        v = st[:, s % 3, 2 * h2:2 * h2 + 2, :]
                        run(v, v, ACT.Copy, st_decayed, scale=GAMMA[2 * hp + h2])
                elif kind == "so" and task[1] == 2 * NS - 1:
                    act.wait_ge(st_read, 2 * NS)
                    run(os_, psum[:, 7, :], ACT.Copy, psum_free[7])
                elif kind == "o":
                    _, h, j = task
                    full(act, task)
                    run(oT[:, 4 * h + j, 0:TP], ps(task)[:, 0:TP], ACT.Copy, free_of(task))
                elif kind == "S":
                    _, h, i = task
                    n = 2 * h + i
                    full(act, task)
                    if n >= 2:
                        act.wait_ge(s_out[n % 2], 16 * (n // 2))
                    run(S_st[:, n % 2, :], ps(task), ACT.Copy, free_of(task))
                    steps.settle()
                    act.dma_start(outs["ret_p"][h, i * P:(i + 1) * P, :], S_st[:, n % 2, :]).then_inc(s_out[n % 2], 16)
                elif kind == "on":
                    h = task[1]
                    if h == 0:
                        read(act, ("soT",))
                        states_stored(act)
                    if h >= 1:
                        full(act, ("on", h - 1))
                    run(sq2, oT[:, 4 * h:4 * h + 4, :], ACT.Square, squares)
                    full(act, task)
                    if h >= 2:
                        act.wait_ge(o_normed, h - 1)
                    run(rstd[:, h % 2, :], ps(task)[:, 0:T], ACT.Sqrt, free_of(task), scale=4.0 / DV, bias=eps_col[:, 2:3])
                elif kind == "g":
                    i = task[1]
                    full(act, task)
                    if i >= 2:
                        act.wait_ge(ret_ready, i - 1)
                    run(gt[:, i % 2, :], ps(task)[:, 0:T], ACT.Tanh, g_tanh, scale=0.5)
                elif kind == "x2_sq":
                    read(act, ("x2", KT - 1))
                    run(sq3, x_res, ACT.Square, squares)
                    norm_root(task, T, 0, D)

            def rows_of(u):
                t, k4 = divmod(u, 2)
                return min(P, T - t * P), t, slice(512 * k4, 512 * k4 + 512)

            act.wait_ge(x_split, 1)
            for u in range(2 * TT):
                n, t, c = rows_of(u)
                act.wait_ge(row_full, u + 1)
                run(xr[0][0:n, t, c], psum[0:n, u % 2, :], ACT.Copy, row_high)
                act.wait_ge(row_rest, u + 1)
                run(xr[1][0:n, t, c], xres[0:n, :], ACT.Copy, row_mid)
            act.wait_ge(router_exp_in, 1)
            run(tmpB[:, 0:TT * 8], tmpB[:, 0:TT * 8], ACT.Exp, router_exp)
            run(yS[:, 1, :], zero_row, ACT.Copy)
            run(hid_z, hid_z, ACT.Copy, hidT_ready)
            run(SwT[:, 1, :], zero_row[:, 0:T], ACT.Copy, scatterT_ready)
            run(tg[:, 0:8], zero_row[:, 0:8], ACT.Copy, y_ready)

            def take_tokens(g, half):
                act.wait_ge(gather_full, g + 1)
                run(XgT[:, half, :, :], psum[:, 0, :].rearrange("p (k s) -> p k s", k=KT), ACT.Copy, tokens_ready)
                act.wait_ge(scatterT_full, g + 1)
                run(SwT[:, half, :], psum[:, 1, 0:T], ACT.Copy, scatterT_ready)

            def chunk_tanh(e):
                act.wait_ge(gate_up_full, e + 1)
                act.wait_ge(hid_ready, e + 1)
                run(tg, psum[:, 2, 0:256], ACT.Tanh, gate_tanh, scale=0.5)

            def chunk_hidden(e):
                act.wait_ge(hidT_full, e + 1)
                run(hT, psum[:, 3, 0:256].rearrange("p (j a s) -> p j a s", j=2, a=2), ACT.Copy, hidT_ready)

            def chunk_out(e, half):
                act.wait_ge(y_full, e + 1)
                run(yS[:, half, :], psum[:, 4:6, :], ACT.Copy, y_ready)

            take_tokens(0, 0)
            with act.Fori(0, EXPERTS, 2) as e0:
                for j in range(2):
                    e = e0 + j
                    chunk_tanh(e)
                    chunk_hidden(e)
                    take_tokens(e0 + (j + 1), 1 - j)
                    chunk_out(e, j)
            n_over = act.value_load(ints[0:1, 0:1], min_val=0, max_val=OVER)
            with act.If(n_over > 0):
                with act.Fori(0, n_over) as j:
                    take_tokens(j + (EXPERTS + 1), 0)
                    chunk_tanh(j + EXPERTS)
                    chunk_hidden(j + EXPERTS)
                    chunk_out(j + EXPERTS, 0)
            with act.Else():
                act.nop()
            act.nop()
            act.wait_ge(x3_ready, 1)
            run(sq3, acc, ACT.Square, squares)
            act.wait_ge(final_sum, 1)
            run(rstd[:, 0, :], psum[:, 0, 0:T], ACT.Sqrt, final_root, scale=1.0 / D, bias=eps_col[:, 0:1])

        @block.vector
        def _(dve):
            V = nc.vector
            steps = Steps(dve, dve_step)
            did, settle = steps.did, steps.settle

            def v(instruction, sem=None):
                did(instruction, sem)
                settle()

            def bc(ap, shape):
                return ap.to_broadcast(list(shape))

            v(V.memset(ones, 1.0), ones_set)
            v(V.memset(eps_col[:, 0:1], EPS))
            v(V.memset(eps_col[:, 1:2], -1.0))
            v(V.memset(eps_col[:, 2:3], 4 * EPS), ones_set)
            dve.wait_ge(const_in, 32)
            for task in order:
                kind = task[0]
                if kind == "mem_sq":
                    read(dve, task)
                    v(V.reciprocal(rstd[:, 0, 0:TP], rstd[:, 0, 0:TP]))
                    for k in range(KT):
                        did(V.scalar_tensor_tensor(memT[:, k, :], memT[:, k, :], cv("norm_mem", k), rstd[:, 0, 0:TP],
                                                   ALU.mult, ALU.mult), mem_normed if k == KT - 1 else None)
                elif kind == "lam":
                    lam, y, s_, s2, c_, t_ = (small[:, 8 * i:8 * i + 8] for i in (7, 0, 1, 2, 3, 4))
                    v(V.tensor_scalar(lam, cvs("lam"), -1.0, None, ALU.mult))
                    v(V.tensor_tensor(y, lam, cvs("lam"), ALU.max), lam_abs)
                    v(V.tensor_scalar(brh[:, 0:2 * KT], chan[:, CH["b_r"] * KT:(CH["b_i"] + 1) * KT], 0.5, None, ALU.mult))
                    dve.wait_ge(lam_exp, 1)
                    v(V.tensor_scalar(t_, y, 2.0, None, ALU.add))
                    v(V.reciprocal(t_, t_))
                    v(V.tensor_tensor(s_, y, t_, ALU.mult))
                    v(V.tensor_tensor(s2, s_, s_, ALU.mult))
                    v(V.tensor_scalar(c_, s2, 1.0 / 15.0, None, ALU.mult))
                    for n in (13, 11, 9, 7, 5, 3):
                        v(V.scalar_tensor_tensor(c_, c_, 1.0 / n, s2, ALU.add, ALU.mult))
                    v(V.scalar_tensor_tensor(c_, c_, 1.0, s_, ALU.add, ALU.mult))
                    v(V.tensor_scalar(lam, lam, 0.0, 4.0, ALU.max, ALU.mult))
                    v(V.scalar_tensor_tensor(sp4, c_, 8.0, lam, ALU.mult, ALU.add), rates)
                elif kind == "x_sq":
                    dve.wait_ge(x_in, 16)
                    read(dve, task)
                    v(V.reciprocal(rstd[:, 1, :], rstd[:, 1, :]))
                    for k in range(KT):
                        did(V.scalar_tensor_tensor(xnT[:, k, :], xT[:, k, :], cv("norm_mix", k), rstd[:, 1, :],
                                                   ALU.mult, ALU.mult), x_normed if k == KT - 1 else None)
                    did(V.memset(uxp[:, :, 0:3], 0.0), pads_zero)
                elif kind == "lg":
                    _, h, l = task
                    full(dve, task)
                    c = stats[:, 2 * h + l:2 * h + l + 1]
                    v(V.tensor_reduce(c, ps(task)[:, 0:TP], AX.X, ALU.max, negate=True))
                    v(V.tensor_scalar(c, c, DK ** -0.5, None, ALU.mult), neg_max)
                    if l == 1:
                        for l in range(2):
                            read(dve, ("lg", h, l))
                            c = stats[:, 8 + 2 * h + l:9 + 2 * h + l]
                            v(V.reciprocal(c, c))
                            v(V.tensor_scalar(prob[:, h % 2, l, :], prob[:, h % 2, l, :], c, None, ALU.mult), prob_normed)
                elif kind == "conv":
                    read(dve, last["ux"])
                    dve.wait_ge(gate_in, 16 * 8)
                    did(V.tensor_copy(conv_st, uxp[:, :, TP:TP + 11]), conv_staged)
                    for j in (3, 2, 1, 0):
                        for k in range(KT):
                            src, dst = uxp[:, k, j:j + TP], uc[:, k, 0:TP]
                            if j == 3:
                                did(V.tensor_scalar(dst, src, cv("w3", k), cv("conv_b", k), ALU.mult, ALU.add))
                            else:
                                did(V.scalar_tensor_tensor(dst, src, cv(f"w{j}", k), dst, ALU.mult, ALU.add))
                        settle()
                    us, ut = uc[:, :, TP:T], tiles(convt, KT)
                    shape = (P, KT, NS)
                    v(V.tensor_tensor(us, uxp[:, :, 3 + TP:3 + T], bc(cvs("w3").unsqueeze(2), shape), ALU.mult))
                    v(V.tensor_tensor(us, us, bc(cvs("conv_b").unsqueeze(2), shape), ALU.add))
                    for j in range(3):
                        v(V.tensor_tensor(ut, sconv[:, :, j, :], bc(cvs(f"w{j}").unsqueeze(2), shape), ALU.mult))
                        v(V.tensor_tensor(us, us, ut, ALU.add), conv_done if j == 2 else None)
                elif kind == "kl":
                    b = task[1]
                    dve.wait_ge(q_bcast, b + 1)
                    dve.wait_ge(kv_in[b % 2], 16 * (b // 2 + 1))
                    v(V.tensor_tensor(prod.rearrange("p (m d) -> p m d", m=2),
                                      kv[:, b % 2, :].rearrange("p (m d) -> p m d", m=2),
                                      bc(qb[:, b % 2, :].unsqueeze(1), (P, 2, D)), ALU.mult))
                    v(V.tensor_reduce(L.rearrange("p (m b h) -> p m b h", m=2, b=NS)[:, :, b, :],
                                      prod.rearrange("p (m h d) -> p m h d", m=2, h=HEADS), AX.X, ALU.add), k_used)
                elif kind == "lru":
                    read(dve, ("i", KT - 1))
                    v(V.tensor_scalar(Rb, Tr, 1.0, None, ALU.add))
                    v(V.reciprocal(Rb, Rb))
                    v(V.scalar_tensor_tensor(Tr, Tr, 0.5, Rb, ALU.mult, ALU.mult))
                    v(V.scalar_tensor_tensor(Ti, Ti, 1.0, uc, ALU.add, ALU.mult))
                    v(V.tensor_scalar(Rb, Rb, 0.5, None, ALU.max), lru_roots_in)
                    dve.wait_ge(lru_roots, 2)
                    v(V.memset(Tr[:, :, 0:1], 0.5))
                    v(V.tensor_tensor(Ti, Tr, Ti, ALU.mult))
                    for k in range(KT):
                        did(V.tensor_tensor_scan(Tr[:, k, 0:TP], Rb[:, k, 0:TP], Ti[:, k, 0:TP], 0.0, ALU.mult, ALU.add))
                    v(V.tensor_tensor(Tr[:, :, TP:T], Rb[:, :, TP:T], slru, ALU.mult))
                    v(V.tensor_tensor(Tr[:, :, TP:T], Tr[:, :, TP:T], Ti[:, :, TP:T], ALU.add))
                    v(V.tensor_copy(lru_st, Tr[:, :, TP - 1:T]), lru_staged)
                elif kind == "gelu":
                    read(dve, last["uy"])
                    v(V.tensor_tensor(Ti, uyT, uyT, ALU.mult))
                    v(V.tensor_scalar(Ti, Ti, 0.044715, 1.0, ALU.mult, ALU.add))
                    v(V.tensor_tensor(Ti, Ti, uyT, ALU.mult), gelu_in)
                    dve.wait_ge(gelu_tanh, 1)
                    v(V.scalar_tensor_tensor(uyT, Ti, 1.0, uyT, ALU.add, ALU.mult))
                    v(V.scalar_tensor_tensor(uyT, uyT, 0.5, Tr, ALU.mult, ALU.mult), lru_ready)
                elif kind in ("rot_q", "rot_k"):
                    x = (qT if kind == "rot_q" else kT).rearrange("p (h i) t -> p h i t", i=2)
                    x1, x2_ = x[:, :, 0, :], x[:, :, 1, :]
                    t1, t2 = (rtmp[:, i * HEADS * T:(i + 1) * HEADS * T].rearrange("p (h t) -> p h t", h=HEADS) for i in (0, 1))
                    cos, sin = (bc(k_(n).unsqueeze(1), (P, HEADS, T)) for n in ("cos", "sin"))
                    read(dve, last["q" if kind == "rot_q" else "k"])
                    full(dve, ("i", KT - 1))
                    v(V.tensor_tensor(t1, x2_, sin, ALU.mult))
                    v(V.tensor_tensor(t2, x1, sin, ALU.mult))
                    v(V.tensor_tensor(x1, x1, cos, ALU.mult))
                    v(V.tensor_tensor(x2_, x2_, cos, ALU.mult))
                    v(V.tensor_tensor(x1, x1, t1, ALU.subtract))
                    v(V.tensor_tensor(x2_, x2_, t2, ALU.add), q_rotated if kind == "rot_q" else k_rotated)
                    if kind == "rot_q":
                        v(V.memset(QM, 0.0))
                        v(V.tensor_copy(diagonal(QMd, KT), qT[:, :, TP:T]))
                elif kind == "sl":
                    v(V.memset(buf("PM"), 0.0))
                    v(V.memset(psum[:, 7, :], 0.0), bank7_zero)
                    full(dve, task)
                    c = stats[0:32, 16:17]
                    v(V.tensor_reduce(c, ps(task)[0:32, 0:TP], AX.X, ALU.max, negate=True))
                    v(V.tensor_scalar(c, c, DK ** -0.5, None, ALU.mult), cache_neg_max)
                    read(dve, task)
                    v(V.reciprocal(stats[0:32, 17:18], stats[0:32, 17:18]))
                    v(V.tensor_scalar(p32[0:32, :], p32[0:32, :], stats[0:32, 17:18], None, ALU.mult), prob_normed)
                elif kind == "spT":
                    full(dve, task)
                    for m in range(2):
                        v(V.tensor_copy(diagonal(PMd + 256 * m, HEADS),
                                        ps(task)[:, 32 * m:32 * m + 32].rearrange("p (b h) -> p h b", h=HEADS)),
                          free_of(task) if m else None)
                elif kind == "scT":
                    full(dve, task)
                    for j in range(2):
                        v(V.tensor_copy(cT.rearrange("p (h j) t -> p h j t", j=2)[:, :, j, TP:T],
                                        ps(task)[:, j * P:(j + 1) * P].rearrange("p (h b) -> p h b", h=HEADS)[:, :, 0:NS]),
                          free_of(task) if j else None)
                    v(V.memset(psum[:, 7, :], 0.0), bank7_zero)
                elif kind == "att":
                    h = task[1]
                    full(dve, task)
                    if h >= 1:
                        full(dve, ("o", h - 1, 3))
                    v(V.tensor_tensor(attT, ps(task)[:, 0:384], k_("dmask")[:, 384 * h:384 * h + 384], ALU.mult),
                      free_of(task))
                elif kind == "sd":
                    s = task[1]
                    b, hp = n_state(s)
                    dve.wait_ge(v_bcast, s + 1)
                    dve.wait_ge(st_decayed, 2 * s + 2)
                    for h2 in range(2):
                        for i in range(2):
                            x = st[:, s % 3, 2 * h2 + i, :]
                            did(V.scalar_tensor_tensor(x, vb[:, s % 2, h2 * DV:(h2 + 1) * DV],
                                                       kT[:, 2 * (2 * hp + h2) + i, TP + b:TP + b + 1], x,
                                                       ALU.mult, ALU.add), st_updated if h2 and i else None)
                elif kind == "soT":
                    full(dve, task)
                    for h in range(HEADS):
                        did(V.tensor_copy(oT[:, 4 * h:4 * h + 4, TP:T],
                                          ps(task).rearrange("p (j c) -> p j c", j=4)[:, :, 32 * h:32 * h + NS]),
                            free_of(task) if h == HEADS - 1 else None)
                elif kind == "on":
                    h = task[1]
                    read(dve, task)
                    r = rstd[:, h % 2, :]
                    v(V.reciprocal(r, r))
                    x = oT[:, 4 * h:4 * h + 4, :]
                    v(V.tensor_tensor(x, x, bc(r.unsqueeze(1), (P, 4, T)), ALU.mult), o_normed)
                elif kind == "g":
                    i = task[1]
                    dve.wait_ge(g_tanh, i + 1)
                    x = gt[:, i % 2, :]
                    v(V.scalar_tensor_tensor(x, x, 1.0, ps(task)[:, 0:T], ALU.add, ALU.mult), free_of(task))
                    v(V.tensor_tensor(oT[:, i, :], oT[:, i, :], x, ALU.mult), ret_ready)
                elif kind == "lru_out":
                    i = task[1]
                    full(dve, task)
                    read(dve, ("ga", i))
                    v(V.scalar_tensor_tensor(merged[:, i, :], merged[:, i, :], 1.0, ps(task)[:, 0:T], ALU.add, ALU.mult),
                      free_of(task))
                elif kind in ("ret_out", "mem_out"):
                    i = task[1]
                    full(dve, task)
                    read(dve, ("gb" if kind == "ret_out" else "gc", i))
                    x = tgate[:, i, :]
                    v(V.scalar_tensor_tensor(x, x, 1.0, ps(task)[:, 0:T], ALU.add, ALU.mult), free_of(task))
                    v(V.tensor_tensor(merged[:, i, :], merged[:, i, :], x, ALU.add), branch_merged)
                elif kind == "x2":
                    i = task[1]
                    full(dve, task)
                    dve.wait_ge(x_again, 16)
                    did(V.scalar_tensor_tensor(x_res[:, i, :], ps(task)[:, 0:T], 0.5, x_res[:, i, :], ALU.mult, ALU.add),
                        free_of(task))
                elif kind == "x2_sq":
                    settle()
                    read(dve, task)
                    v(V.reciprocal(rstd[:, 0, :], rstd[:, 0, :]))
                    for k in range(KT):
                        did(V.scalar_tensor_tensor(xnT[:, k, :], x_res[:, k, :], cv("norm_ffn", k), rstd[:, 0, :],
                                                   ALU.mult, ALU.mult), x2_normed if k == KT - 1 else None)

            settle()
            states_stored(dve)
            for x in xr:
                did(V.memset(x[:, 2, :], 0.0))
            v(V.memset(zero_row, 0.0))
            v(V.memset(lgt, 0.0))
            v(V.memset(hid_z, 0.0), x_split)
            for u in range(2 * TT):
                t, k4 = divmod(u, 2)
                n, c = min(P, T - t * P), slice(512 * k4, 512 * k4 + 512)
                dve.wait_ge(row_high, u + 1)
                v(V.tensor_tensor(xres[0:n, :], psum[0:n, u % 2, :], xr[0][0:n, t, c], ALU.subtract), row_rest)
                dve.wait_ge(row_mid, u + 1)
                v(V.tensor_tensor(xr[2][0:n, t, c], xres[0:n, :], xr[1][0:n, t, c], ALU.subtract))

            dve.wait_ge(logits_full, 1)
            lgp = psum[:, 2, 0:192].rearrange("p (t c) -> p t c", t=TT)
            v(V.tensor_copy(lgt[:, 0:2, :], lgp[:, 0:2, 0:NLOG]))
            v(V.tensor_copy(lgt[0:T - 2 * P, 2:3, :], lgp[0:T - 2 * P, 2:3, 0:NLOG]))
            G, E8 = GROUPS, PER_GROUP
            c32, c8 = k_("count32"), k_("count8")

            def view(base, at, n):
                return base[:, at:at + TT * n].rearrange("p (t n) -> p t n", t=TT)

            def first_max(onehot, peak, x, n, scratch):
                v(V.tensor_reduce(peak, x, AX.X, ALU.max))
                v(V.tensor_tensor(onehot, x, bc(peak, (P, TT, n)), ALU.is_lt))
                v(V.scalar_tensor_tensor(onehot, onehot, 64.0, bc(c32[:, 0:n].unsqueeze(1), (P, TT, n)), ALU.mult, ALU.add))
                v(V.tensor_reduce(scratch, onehot, AX.X, ALU.min))
                v(V.tensor_tensor(onehot, onehot, bc(scratch, (P, TT, n)), ALU.is_equal))

            oh_g, oh_1, oh_2 = view(tmpC, 0, G), view(tmpC, 16, E8), view(tmpC, 48, E8)
            peak, pos, sel = view(tmpC, 80, 1), view(tmpC, 84, 1), view(tmpC, 96, E8)
            sel2, gs, w1, w2, sgm = view(tmpC, 128, E8), view(tmpC, 160, 1), view(tmpC, 164, 1), view(tmpC, 168, 1), view(tmpC, 172, 1)
            pk1, pk2 = view(tmpC, 176, 1), view(tmpC, 180, 1)
            big = tiles(tmpD, TT)
            lg_g = lgt[:, :, 0:G]
            ex = view(tmpB, 0, 8)
            first_max(oh_g, peak, lg_g, G, pos)
            v(V.tensor_tensor(ex[:, :, 0:G], lg_g, bc(peak, (P, TT, G)), ALU.subtract))
            gsel = tmpD[:, 0:TT * EXPERTS].rearrange("p (t g e) -> p t g e", t=TT, g=G)
            for g in range(G):
                src = lgt[:, :, G + g * E8:G + (g + 1) * E8]
                if g == 0:
                    v(V.tensor_tensor(sel, src, bc(oh_g[:, :, 0:1], (P, TT, E8)), ALU.mult))
                else:
                    v(V.tensor_tensor(sel2, src, bc(oh_g[:, :, g:g + 1], (P, TT, E8)), ALU.mult))
                    v(V.tensor_tensor(sel, sel, sel2, ALU.add))
            first_max(oh_1, pk1, sel, E8, pos)
            v(V.scalar_tensor_tensor(sel2, oh_1, -3.0e38, sel, ALU.mult, ALU.add))
            first_max(oh_2, pk2, sel2, E8, pos)
            v(V.tensor_tensor(ex[:, :, 4:5], pk2, pk1, ALU.subtract))
            v(V.memset(ex[:, :, 5:8], 0.0), router_exp_in)
            dve.wait_ge(router_exp, 1)
            v(V.tensor_reduce(gs, ex[:, :, 0:G], AX.X, ALU.add))
            v(V.tensor_scalar(sgm, ex[:, :, 4:5], 1.0, 2.0, ALU.add, ALU.mult))
            v(V.tensor_tensor(gs, gs, sgm, ALU.mult))
            v(V.reciprocal(w1, gs))
            v(V.tensor_tensor(w2, w1, ex[:, :, 4:5], ALU.mult))
            v(V.tensor_tensor(sel, oh_1, oh_2, ALU.add))
            v(V.tensor_tensor(sel, sel, bc(k_("valid").unsqueeze(2), (P, TT, E8)), ALU.mult))
            v(V.tensor_tensor(oh_1, oh_1, bc(w1, (P, TT, E8)), ALU.mult))
            v(V.tensor_tensor(oh_2, oh_2, bc(w2, (P, TT, E8)), ALU.mult))
            v(V.tensor_tensor(sel2, oh_1, oh_2, ALU.add))
            for g in range(G):
                v(V.tensor_tensor(M01[:, :, g * E8:(g + 1) * E8], sel, bc(oh_g[:, :, g:g + 1], (P, TT, E8)), ALU.mult),
                  masks_ready if g == G - 1 else None)
            for g in range(G):
                v(V.tensor_tensor(Wc[:, :, g * E8:(g + 1) * E8], sel2, bc(oh_g[:, :, g:g + 1], (P, TT, E8)), ALU.mult))
            dve.wait_ge(ranks_full, 1)
            rkp = psum[:, 3, 0:192].rearrange("p (t c) -> p t c", t=TT)[:, :, 0:EXPERTS]
            R32 = tmpD[:, 0:TT * EXPERTS].rearrange("p (t e) -> p t e", t=TT)
            v(V.scalar_tensor_tensor(R32, rkp, 1.0, M01, ALU.add, ALU.mult))
            v(V.tensor_scalar(Rc[:, :, 0:EXPERTS], R32, -1.0, None, ALU.add))
            cnt, ext, cum, exc, tm = (ov[:, 32 * i:32 * i + 32] for i in range(5))
            ej, cx, vj, kj = (ov[:, 160 + 8 * i:168 + 8 * i] for i in range(4))
            big = tmpA[:, 0:OVER * EXPERTS].rearrange("p (j e) -> p j e", j=OVER)
            oh_j = tmpA[:, OVER * EXPERTS:2 * OVER * EXPERTS].rearrange("p (j e) -> p j e", j=OVER)
            sh = (P, OVER, EXPERTS)
            v(V.tensor_copy(cnt, psum[:, 3, 192:192 + EXPERTS]))
            v(V.tensor_scalar(ext, cnt, float(SLOTS), None, ALU.is_gt))
            for k in range(2, (T - 1) // SLOTS + 1):
                v(V.tensor_scalar(tm, cnt, float(SLOTS * k), None, ALU.is_gt))
                v(V.tensor_tensor(ext, ext, tm, ALU.add))
            v(V.tensor_tensor_scan(cum, ones[:, 0:EXPERTS], ext, 0.0, ALU.mult, ALU.add))
            v(V.tensor_tensor(exc, cum, ext, ALU.subtract))
            v(V.tensor_tensor(big, bc(cum.unsqueeze(1), sh), bc(c8.unsqueeze(2), sh), ALU.is_le))
            v(V.tensor_reduce(ej, big, AX.X, ALU.add))
            v(V.tensor_tensor(oh_j, bc(c32.unsqueeze(1), sh), bc(ej.unsqueeze(2), sh), ALU.is_equal))
            v(V.tensor_tensor(big, oh_j, bc(exc.unsqueeze(1), sh), ALU.mult))
            v(V.tensor_reduce(cx, big, AX.X, ALU.add))
            v(V.tensor_tensor(kj, c8, cx, ALU.subtract))
            v(V.tensor_scalar(kj, kj, float(SLOTS), float(SLOTS + 1), ALU.mult, ALU.add))
            for t in range(TT):
                v(V.tensor_tensor(big, oh_j, bc(R32[:, t:t + 1, :], sh), ALU.mult))
                v(V.tensor_reduce(vj, big, AX.X, ALU.add))
                v(V.tensor_tensor(Rc[:, t, EXPERTS:COLS], vj, kj, ALU.subtract))
                v(V.tensor_tensor(big, oh_j, bc(Wc[:, t:t + 1, 0:EXPERTS], sh), ALU.mult))
                v(V.tensor_reduce(Wc[:, t, EXPERTS:COLS], big, AX.X, ALU.add))
            v(V.tensor_scalar(ej, ej, float(EXPERTS - 1), None, ALU.min))
            v(V.tensor_copy(ints[:, 0:8], cum[:, EXPERTS - 1:EXPERTS].to_broadcast([P, 8])))
            v(V.tensor_copy(ints[:, 8:16], ej), routed)
            v(V.memset(hid, 0.0), hid_ready)
            v(V.memset(acc[:, 0:4, :], 0.0), scatter_added)
            v(V.memset(acc[:, 4:8, :], 0.0), scatter_added)

            def build(g, col, half):
                if not isinstance(g, int):
                    dve.wait_ge(onehot_built, g)
                col = slice(col, col + 1) if isinstance(col, int) else bass.ds(col, 1)
                sh3 = (P, TT, P)
                V.tensor_tensor(eq, bc(k_("slot2").unsqueeze(1), sh3), bc(Rc[:, :, col], sh3),
                                ALU.is_equal).then_inc(eq_built, 1)
                dve.wait_ge(eq_built, g + 1)
                V.tensor_copy(Sb[:, half, :, :], eq[:, :, 0:SLOTS]).then_inc(dve_step, 1)
                V.tensor_tensor(Sw[:, half, :, :], eq, bc(Wc[:, :, col], sh3), ALU.mult).then_inc(onehot_built, 1)

            def hidden(e):
                dve.wait_ge(gate_tanh, e + 1)
                V.scalar_tensor_tensor(tmid, tg, 1.0, psum[:, 2, 0:256], ALU.add, ALU.mult).then_inc(swish_mid, 1)
                dve.wait_ge(swish_mid, e + 1)
                V.tensor_tensor(hid, tmid, psum[:, 2, 256:512], ALU.mult).then_inc(hid_ready, 1)

            def add_scattered(n):
                for d in range(KT):
                    dve.wait_ge(scatter_full, n * KT + (d + 1))
                    V.tensor_tensor(acc[:, d, :], acc[:, d, :], psum[:, 6 + d % 2, 0:T], ALU.add).then_inc(
                        scatter_added, 1)
                dve.wait_ge(scatter_added, n * KT + (KT + 2))

            settle()
            build(0, 0, 0)
            dve.wait_ge(onehot_built, 1)
            build(1, 1, 1)
            with dve.Fori(0, EXPERTS, 2) as e0:
                for j in range(2):
                    hidden(e0 + j)
                    add_scattered(e0 + j)
                    build(e0 + (j + 2), e0 + (j + 2), j)
            add_scattered(EXPERTS)
            n_over = dve.value_load(ints[0:1, 0:1], min_val=0, max_val=OVER)
            with dve.If(n_over > 0):
                with dve.Fori(0, n_over) as j:
                    dve.wait_ge(scatterT_full, j + (EXPERTS + 1))
                    build(j + (EXPERTS + 2), j + EXPERTS, 0)
                    hidden(j + EXPERTS)
                    add_scattered(j + (EXPERTS + 1))
            with dve.Else():
                dve.nop()
            dve.nop()
            V.tensor_tensor(acc, acc, x_res, ALU.add).then_inc(x3_ready, 1)
            dve.wait_ge(final_root, 1)
            V.reciprocal(rstd[:, 0, :], rstd[:, 0, :]).then_inc(final_root, 1)
            dve.wait_ge(final_root, 2)
            for k in range(KT):
                V.scalar_tensor_tensor(acc[:, k, :], acc[:, k, :], cv("norm_final", k), rstd[:, 0, :],
                                       ALU.mult, ALU.mult).then_inc(final_normed, 1)


_OUTS = {
    "y": (D, T), "conv_keep": (NS, 2, D), "conv_new": (P, KT, 11), "lru": (P, KT, 9),
    "ret_p": (HEADS, DK, DV), "ret_s": (NS, HEADS, DK, DV), "mem_k": (TP, D), "mem_v": (TP, D),
}


def kernel(**inputs):
    import concourse.bacc as bacc
    from concourse.bass_utils import run_bass_kernel_spmd

    x = {k: np.asarray(v) for k, v in inputs.items()}
    f = np.ascontiguousarray
    cols = lambda a: a.reshape(KT, P).T
    names = ["norm_mix", "norm_ffn", "norm_mem", None, "conv_b", "b_r", "b_i", "lru_lambda"]
    chan = [cols(x[n][0]) if n else cols(x["norm_final"]) for n in names]
    chan += [cols(x["conv_w"][0, j]) for j in range(4)]
    const, const_at = shape_constants()
    arrays = {
        "const": const,
        "chan": f(np.concatenate(chan, axis=1)),
        "xT": f(np.concatenate([x["x_prompt"][0], x["x_sample"][:, 0]], axis=0).T),
        "memT": f(x["mem_prompt"][0].T),
        "sconv": f(x["state_conv"][0].reshape(NS, 3, KT, P).transpose(3, 2, 1, 0).reshape(P, -1)),
        "slru": f(x["state_lru"][0].reshape(NS, KT, P).transpose(2, 1, 0).reshape(P, -1)),
        "router": f(np.concatenate([x["w_grp"][0], x["w_exp_router"][0].transpose(1, 0, 2).reshape(D, EXPERTS)], axis=1)),
        "rbias": f(np.concatenate([x["b_grp"][0], x["b_exp_router"][0].reshape(-1)])[None]),
        "state_conv": x["state_conv"][0], "state_ret": x["state_ret"][0],
        "cache_mem_k": x["cache_mem_k"][0], "cache_mem_v": x["cache_mem_v"][0],
    }
    for n in ("w_in", "w_mem_kv", "w_r", "w_i", "w_branch_lru", "w_branch_ret", "w_branch_mem", "w_out", "w_gate",
              "w_up", "w_down"):
        arrays[n] = x[n][0]
    nc = bacc.Bacc("TRN2", target_bir_lowering=False, num_devices=1)
    dram = {n: nc.dram_tensor(f"in_{n}", a.shape, F32, kind="ExternalInput").ap() for n, a in arrays.items()}
    outs = {n: nc.dram_tensor(f"out_{n}", s, F32, kind="ExternalOutput").ap() for n, s in _OUTS.items()}
    build_program(nc, dram, outs, const_at)
    r = run_bass_kernel_spmd(nc, [{f"in_{n}": a for n, a in arrays.items()}], core_ids=[0]).results[0]
    o = {n: np.asarray(r[f"out_{n}"]) for n in _OUTS}
    y = o["y"].T
    rows = lambda a: a.transpose(2, 1, 0).reshape(a.shape[2], D)
    conv, lru = rows(o["conv_new"]), rows(o["lru"])
    conv_s = np.concatenate([o["conv_keep"], conv[3:, None, :]], axis=1)
    return (f(y[:TP])[None], f(y[TP:])[:, None], f(conv[:3])[None, None], f(lru[:1])[None], o["ret_p"][None, None],
            o["mem_k"].reshape(1, 1, TP, HEADS, DK), o["mem_v"].reshape(1, 1, TP, HEADS, DK), f(conv_s)[None],
            f(lru[1:])[None], o["ret_s"][None])
```

```python
from contextlib import ExitStack

import numpy as np
import concourse.bass as bass
from concourse import mybir

F32 = mybir.dt.float32
BF16 = mybir.dt.bfloat16
I32 = mybir.dt.int32
ACT = mybir.ActivationFunctionType
ALU = mybir.AluOpType
AX = mybir.AxisListType

P = 128
D = 1024
KT = D // P
TP, NS = 256, 8
T = TP + NS
HEADS, DK, DV = 4, 256, 512
VT = HEADS * DV // P
EPS = 1e-6
EXPERTS, GROUPS, PER_GROUP, FF = 32, 4, 8, 512
NLOG = GROUPS + EXPERTS
SLOTS = 64
OVER = (2 * T) // (SLOTS + 1)
COLS = EXPERTS + OVER + 4
TT = 3
CHUNK = 2048
RING = 6
RING1 = 5
GAMMA = [float(1.0 - 2.0 ** (-5.0 - h)) for h in range(HEADS)]
PAST_LEN = 2048
ROPE_BASE = 10000.0

OFF = {"ux": 0, "uy": 1024, "q": 2048, "k": 3072, "v": 4096, "g": 6144, "mq": 8192,
       "ga": 9216, "gb": 10240, "gc": 11264}
CH = {n: i for i, n in enumerate(["norm_mix", "norm_ffn", "norm_mem", "norm_final", "conv_b", "b_r", "b_i",
                                  "lam", "w0", "w1", "w2", "w3"])}


def shape_constants():
    f = np.float32
    half = DK // 2
    inv = np.power(f(ROPE_BASE), -np.linspace(0.0, 1.0, half, dtype=f)).astype(f)
    pos = np.concatenate([np.arange(TP), np.full(NS, PAST_LEN)]).astype(f)
    ang = (inv[:, None] * pos[None, :]).astype(f)
    log_g = np.log1p(-(2.0 ** (-5.0 - np.arange(HEADS))))
    p = np.arange(P)
    mask = np.zeros((P, HEADS, 384))
    for h in range(HEADS):
        n = np.arange(TP)
        mask[:, h, :TP] = np.where(n[None] >= p[:, None], np.exp(np.maximum(n[None] - p[:, None], 0) * log_g[h]), 0)
        mask[:, h, TP:] = mask[:, h, :P]
    kdec = np.zeros((P, 2, HEADS))
    for mt in range(2):
        kdec[:, mt, :] = np.exp((TP - 1 - (mt * P + p))[:, None] * log_g[None])
    valid = np.ones((P, TT))
    valid[T - 2 * P:, 2] = 0
    parts = {
        "cos": np.cos(ang), "sin": np.sin(ang), "dmask": mask.reshape(P, -1),
        "ident": np.eye(P), "kdec": kdec.reshape(P, -1), "before": (p[:, None] < p[None, :]).astype(f), "valid": valid,
        "slot": np.tile(np.arange(SLOTS), (P, 1)), "count32": np.tile(np.arange(EXPERTS), (P, 1)),
        "count8": np.tile(np.arange(OVER), (P, 1)),
    }
    at, cols, off = {}, [], 0
    for name, a in parts.items():
        at[name] = (off, off + a.shape[1])
        off += a.shape[1]
        cols.append(a.astype(f))
    return np.ascontiguousarray(np.concatenate(cols, axis=1)), at


STAGES = ["load", "mem", "mq", "ux", "uy", "q", "k", "v", "rows", "ga", "gc", "gb", "g", "ret", "x2", "route", "moe",
          "end"]
ARENA = 53192
NCONST = shape_constants()[0].shape[1]
NROPE, NMASK = 2 * T, HEADS * 384
BUFFERS = {
    "rope": (NROPE, "load", "v"),
    "dmask": (NMASK, "load", "gc"),
    "const": (NCONST - NROPE - NMASK, "load", "end"),
    "ones": (P, "load", "end"),
    "chan": (12 * KT, "load", "end"),
    "xT": (KT * T, "load", "mem"),
    "x": (KT * T, "gb", "end"),
    "xnT": (KT * T, "load", "route"),
    "rstd": (2 * T, "load", "end"),
    "small": (KT * 8, "load", "q"),
    "sp4": (KT, "load", "q"),
    "brh": (2 * KT, "load", "q"),
    "stats": (64, "load", "v"),
    "eps_col": (8, "load", "end"),
    "memT": (KT * TP, "load", "mem"),
    "sq": (KT * T, "load", "mem"),
    "wr": (KT * P, "load", "q"),
    "wi": (KT * P, "load", "q"),
    "sconv": (KT * 3 * NS, "load", "uy"),
    "slru": (KT * NS, "load", "v"),
    "mk_rows": (2 * D, "mem", "mq"),
    "mv_rows": (2 * D, "mem", "uy"),
    "mkT": (KT * TP, "mem", "uy"),
    "mqT": (KT * T, "mq", "uy"),
    "mqs_rows": (D, "mq", "k"),
    "mq_row0": (D, "mq", "k"),
    "qb": (2 * D, "mq", "k"),
    "kv": (2 * 2 * D, "mq", "v"),
    "prod": (2 * D, "mq", "k"),
    "L": (64, "mq", "k"),
    "prob": (4 * TP, "ux", "uy"),
    "probT": (2 * TP, "ux", "uy"),
    "cT": (KT * T, "ux", "gc"),
    "uxp": (KT * 272, "ux", "uy"),
    "uc": (KT * T, "uy", "v"),
    "convt": (64, "uy", "uy"),
    "Tr": (KT * T, "q", "rows"),
    "Ti": (KT * T, "q", "rows"),
    "Rb": (KT * T, "q", "v"),
    "uyT": (KT * T, "uy", "ga"),
    "lru_st": (KT * 16, "ux", "end"),
    "conv_st": (KT * 16, "ux", "end"),
    "qT": (KT * T, "q", "gc"),
    "kT": (KT * T, "k", "gc"),
    "rtmp": (HEADS * 2 * T, "k", "v"),
    "vT": (VT * T, "v", "rows"),
    "v_rows": (2 * HEADS * DV, "rows", "gc"),
    "k_rows": (2 * D, "v", "gc"),
    "vs_rows": (HEADS * DV, "rows", "gc"),
    "v_row0": (D, "rows", "gc"),
    "vb": (2 * D, "rows", "gc"),
    "st": (3 * 4 * DV, "rows", "gc"),
    "p32": (TP, "k", "k"),
    "PM": (512, "k", "v"),
    "cs": (TP, "k", "rows"),
    "QM": (KT * 64, "k", "gc"),
    "attT": (384, "rows", "gc"),
    "oT": (VT * T, "ga", "ret"),
    "S_st": (2 * DV, "ga", "gb"),
    "os": (DV, "ga", "gb"),
    "merged": (KT * T, "ga", "x2"),
    "tgate": (KT * T, "gc", "x2"),
    "gt": (2 * T, "g", "g"),
    "sq2": (2 * 4 * T, "gb", "gb"),
    "sq3": (KT * T, "x2", "end"),
    "rout": (KT * NLOG, "load", "end"),
    "rbias": (NLOG, "load", "end"),
    "last_gate_up": (4 * CHUNK, "x2", "end"),
    "filler": (24, "route", "end"),
    "xr0": (TT * D // 2, "route", "end"),
    "xr1": (TT * D // 2, "route", "end"),
    "xr2": (TT * D // 2, "route", "end"),
    "xrow": (2 * 512, "route", "route"),
    "xres": (2 * 512, "route", "route"),
    "lgT": (T, "route", "route"),
    "tables16": (P, "route", "end"),
    "lgt": (TT * NLOG, "route", "end"),
    "Rc": (TT * COLS, "route", "end"),
    "Wc": (TT * COLS, "route", "end"),
    "M01": (TT * EXPERTS // 2, "route", "end"),
    "tmpA": (2 * OVER * EXPERTS, "route", "end"),
    "tmpB": (TT * 64, "route", "end"),
    "tmpC": (TT * 64, "route", "end"),
    "tmpD": (TT * 64, "route", "end"),
    "ov": (512, "route", "end"),
    "ints": (24, "route", "end"),
    "eq": (TT * P, "route", "end"),
    "Sw": (TT * P, "route", "end"),
    "Sb": (TT * P // 2, "route", "end"),
    "XgT": (2 * KT * SLOTS, "moe", "end"),
    "SwT": (T, "route", "end"),
    "tg": (256, "moe", "end"),
    "hid": (256, "moe", "end"),
    "hT": (2 * 256, "moe", "end"),
    "yS": (D, "route", "end"),
    "tmid": (256, "moe", "end"),
}


def place_buffers():
    stage = {s: i for i, s in enumerate(STAGES)}
    names = list(BUFFERS)

    def place(order):
        held = [(0, RING1 * CHUNK, 0, stage["end"]), (RING1 * CHUNK, 2 * RING * CHUNK, stage["ret"], stage["end"])]
        found = {}
        for name in order:
            size, first, last = BUFFERS[name]
            a, b, at = stage[first], stage[last], 0
            size = (size + 7) // 8 * 8
            for lo, hi, x, y in sorted(held):
                if b < x or y < a or hi <= at:
                    continue
                if lo >= at + size:
                    break
                at = hi
            held.append((at, at + size, a, b))
            found[name] = at
        return found, max(h[1] for h in held)

    for seed in range(5000):
        rng = np.random.default_rng(seed)
        power, spread = rng.uniform(0, 2.5), rng.standard_normal(len(names)) * rng.uniform(0, 1)
        weight = {n: BUFFERS[n][0] * (stage[BUFFERS[n][2]] - stage[BUFFERS[n][1]] + 1) ** power * np.exp(z)
                  for n, z in zip(names, spread)}
        found, top = place(sorted(names, key=lambda n: -weight[n]))
        if top <= ARENA:
            return found
    raise AssertionError("the buffers do not fit")


def weave(main, side):
    out, n = [], 0
    for i, m in enumerate(main):
        out.append(m)
        while n * len(main) < (i + 1) * len(side):
            out.append(side[n])
            n += 1
    return out


def tensor_order():
    t = lambda kind, n: [(kind, i) for i in range(n)]
    heads = range(HEADS)
    lg = [[("lg", h, 0), ("lg", h, 1)] for h in heads]
    pv = [[("pT", h), ("pv", h, 0), ("pv", h, 1)] for h in heads]
    attn = lg[0] + lg[1] + pv[0] + lg[2] + pv[1] + lg[3] + pv[2] + pv[3]
    gates = [x for n in range(KT) for x in (("r", n), ("i", n))]
    kl = t("kl", NS)
    cache = [("sl",), ("spT",)] + t("sc", NS)
    krows = [("kr", m, q) for m in range(2) for q in range(2)]
    v = t("v", VT)
    vrows = t("vs", 4) + [("vr", m, q) for q in range(4) for m in range(2)]
    ret = []
    for h in heads:
        ret += [("att", h)] + [("o", h, j) for j in range(4)] + [("S", h, i) for i in range(2)]
    so = [("sd", 0)]
    for s in range(2 * NS):
        so += ([("sd", s + 1)] if s + 1 < 2 * NS else []) + [("so", s)]
    branches = t("ga", 8) + t("lru_out", 8) + t("gc", 8) + t("mem_out", 8)
    onorm = [("soT",), ("oq", 0), ("oq", 1), ("on", 0), ("oq", 2), ("on", 1), ("oq", 3), ("on", 2), ("on", 3)]
    return (
        [("mem_sq",)] + t("mk", 8)[:2] + [("xq",)] + t("mk", 8)[2:4] + [("x_sq",), ("lam",)] + t("mk", 8)[4:]
        + weave(t("mv", 8), t("mkT", 4)) + t("mq", 8) + t("mqs", 2)
        + weave(t("ux", 8), weave(attn[:11], kl[:2])) + [("conv",)] + weave(t("uy", 8), weave(attn[11:], kl[2:5]))
        + weave(t("q", 8), weave(gates, kl[5:])) + weave(t("k", 8)[:3], cache[:2]) + [("rot_q",)]
        + weave(t("k", 8)[3:], cache[2:5]) + [("rot_k",), ("lru",)]
        + weave(v[:6], cache[5:]) + [("lru_root",), ("gelu",)] + weave(v[6:12], krows) + [("gelu_tanh",)] + v[12:]
        + [("scT",)] + vrows + ret[:1]
        + weave(weave(branches, ret[1:]), so)
        + weave(t("gb", 8), onorm) + t("g", 16) + t("ret_out", 8) + t("x2", 8) + [("x2_sq",)]
    )


NO_PSUM = {"oq", "xq", "lam", "sd", "conv", "kl", "lru", "lru_root", "gelu", "gelu_tanh", "rot_q", "rot_k"}
PROJECTIONS = {"mk", "mv", "mq", "ux", "uy", "q", "k", "v", "g", "ga", "gb", "gc", "lru_out", "ret_out",
               "mem_out", "x2"}


class Steps:

    def __init__(self, engine, default):
        self.engine, self.default, self.count, self.last = engine, default, {}, None

    def did(self, instruction, sem=None):
        sem = self.default if sem is None else sem
        if isinstance(sem, tuple):
            sem, count = sem
        else:
            count = self.count[id(sem)] = self.count.get(id(sem), 0) + 1
        instruction.then_inc(sem, 1)
        self.last = (sem, count)

    def settle(self):
        if self.last:
            self.engine.wait_ge(*self.last)


def build_program(nc, dram, outs, const_at):
    order = tensor_order()
    where, uses, turn = {}, [0] * 8, {"proj": 0, "side": 0}
    for task in order:
        kind = task[0]
        if kind in NO_PSUM:
            continue
        if kind in ("sc", "so"):
            if task[1] == 0:
                uses[7] += 1
            where[task] = (7, uses[7] - 1)
            continue
        if kind in PROJECTIONS:
            bank = turn["proj"] % 4
            turn["proj"] += 1
        else:
            bank = 4 + turn["side"] % 3
            turn["side"] += 1
        where[task] = (bank, uses[bank])
        uses[bank] += 1

    def wide(w, col, row=0):
        return w[row:row + D, col:col + 256].rearrange("(k p) n -> p k n", p=P)

    chunks, chunk_of, last_task = [], {}, []

    def chunk(kind, c, ap):
        chunk_of[(kind, c)] = len(chunks)
        chunks.append(ap)
        last_task.append(("ret_out" if kind == "ret_out2" else kind, 2 * c + 1))

    seen = set()
    for task in order:
        kind = task[0]
        if kind not in PROJECTIONS or task[1] % 2:
            continue
        c = task[1] // 2
        if kind in ("mk", "mv"):
            chunk(kind, c, wide(dram["w_mem_kv"], (0 if kind == "mk" else D) + c * 256))
        elif kind == "lru_out":
            chunk(kind, c, wide(dram["w_branch_lru"], c * 256))
        elif kind == "mem_out":
            chunk(kind, c, wide(dram["w_branch_mem"], c * 256))
        elif kind == "x2":
            chunk(kind, c, wide(dram["w_out"], c * 256))
        elif kind == "ret_out":
            chunk(kind, c, wide(dram["w_branch_ret"], c * 256))
            chunk("ret_out2", c, wide(dram["w_branch_ret"], c * 256, D))
        else:
            chunk(kind, c, wide(dram["w_in"], OFF[kind] + c * 256))
    NCH = len(chunks)
    ring_uses = [len(range(s, NCH, RING1)) if s < RING1 else 0 for s in range(RING)]

    with ExitStack() as ctx:
        place_of = place_buffers()
        arena = ctx.enter_context(nc.sbuf_tensor("arena", [P, ARENA], F32))

        def buf(name):
            at = place_of[name]
            return arena[:, at:at + BUFFERS[name][0]]

        def tiles(ap, n):
            return ap.rearrange("p (k n) -> p k n", k=n)

        ring = arena[:, 0:2 * RING * CHUNK]
        slot = tiles(ring, 2 * RING)
        last_gate_up = tiles(buf("last_gate_up"), 4)
        const = buf("const")

        def k_(name):
            a, b = const_at[name]
            home, first = {"cos": ("rope", 0), "sin": ("rope", 0), "dmask": ("dmask", NROPE)}.get(
                name, ("const", NROPE + NMASK))
            return buf(home)[:, a - first:b - first]

        ident = k_("ident")
        ones = buf("ones")
        chan = buf("chan")
        cv = lambda name, kt: chan[:, CH[name] * KT + kt:CH[name] * KT + kt + 1]
        cvs = lambda name: chan[:, CH[name] * KT:(CH[name] + 1) * KT]
        xT = tiles(buf("xT"), KT)
        x_res = tiles(buf("x"), KT)
        xnT = tiles(buf("xnT"), KT)
        rstd = tiles(buf("rstd"), 2)
        small = buf("small")
        sp4 = buf("sp4")
        brh = buf("brh")
        stats = buf("stats")
        eps_col = buf("eps_col")
        memT = tiles(buf("memT"), KT)
        sq = tiles(buf("sq"), KT)
        wr = tiles(buf("wr"), KT)
        wi = tiles(buf("wi"), KT)
        sconv = buf("sconv").rearrange("p (k j b) -> p k j b", k=KT, j=3)
        slru = tiles(buf("slru"), KT)
        mk_rows = tiles(buf("mk_rows"), 2)
        mv_rows = tiles(buf("mv_rows"), 2)
        mkT = tiles(buf("mkT"), KT)
        mqT = tiles(buf("mqT"), KT)
        mqs_rows = buf("mqs_rows")
        mq_row0 = buf("mq_row0")
        qb = tiles(buf("qb"), 2)
        kv = tiles(buf("kv"), 2)
        prod = buf("prod")
        L = buf("L")
        prob = buf("prob").rearrange("p (a l m) -> p a l m", a=2, l=2)
        probT = tiles(buf("probT"), 2)
        cT = tiles(buf("cT"), KT)
        uxp = tiles(buf("uxp"), KT)
        uc = tiles(buf("uc"), KT)
        convt = buf("convt")
        Tr = tiles(buf("Tr"), KT)
        Ti = tiles(buf("Ti"), KT)
        Rb = tiles(buf("Rb"), KT)
        uyT = tiles(buf("uyT"), KT)
        lru_st = tiles(buf("lru_st"), KT)[:, :, 0:9]
        conv_st = tiles(buf("conv_st"), KT)[:, :, 0:11]
        qT = tiles(buf("qT"), KT)
        kT = tiles(buf("kT"), KT)
        rtmp = buf("rtmp")
        vT = tiles(buf("vT"), VT)
        v_rows = tiles(buf("v_rows"), 2)
        k_rows = tiles(buf("k_rows"), 2)
        vs_rows = buf("vs_rows")
        v_row0 = buf("v_row0")
        vb = tiles(buf("vb"), 2)
        st = buf("st").rearrange("p (s i v) -> p s i v", s=3, i=4)
        p32 = buf("p32")
        PM = buf("PM").rearrange("p (m h b c) -> p m h b c", m=2, h=HEADS, b=NS)
        PMd = place_of["PM"]
        cs = buf("cs")
        QM = buf("QM").rearrange("p (k b c) -> p k b c", k=KT, b=NS)
        QMd = place_of["QM"]
        attT = buf("attT")
        oT = tiles(buf("oT"), VT)
        S_st = tiles(buf("S_st"), 2)
        os_ = buf("os")
        merged = tiles(buf("merged"), KT)
        tgate = tiles(buf("tgate"), KT)
        gt = tiles(buf("gt"), 2)
        sq2 = buf("sq2").rearrange("p (a k n) -> p a k n", a=2, k=4)
        sq3 = tiles(buf("sq3"), KT)
        rout = tiles(buf("rout"), KT)
        rbias = buf("rbias")
        xr = [buf(f"xr{i}").bitcast(BF16).rearrange("p (t d) -> p t d", t=TT) for i in range(3)]
        xrow = tiles(buf("xrow"), 2)
        xres = tiles(buf("xres"), 2)
        filler = buf("filler")
        lgT = buf("lgT")
        ones16, before16 = (buf("tables16").bitcast(BF16)[:, a:a + P] for a in (0, P))
        lgt = tiles(buf("lgt"), TT)
        Rc = tiles(buf("Rc"), TT)
        Wc = tiles(buf("Wc"), TT)
        M01 = tiles(buf("M01").bitcast(BF16), TT)
        tmpA = buf("tmpA")
        tmpB = buf("tmpB")
        tmpC = buf("tmpC")
        tmpD = buf("tmpD")
        ov = buf("ov")
        ints = buf("ints").bitcast(I32)
        eq = tiles(buf("eq"), TT)
        Sw = tiles(buf("Sw"), TT)
        Sb = tiles(buf("Sb").bitcast(BF16), TT)
        XgT = buf("XgT").rearrange("p (a k s) -> p a k s", a=2, k=KT)
        SwT = buf("SwT")
        tg = buf("tg")
        hid = buf("hid")
        hT = buf("hT").rearrange("p (e j a s) -> p e j a s", e=2, j=2, a=2)
        yS = buf("yS")
        y_out = sq3
        tmid = buf("tmid")

        def diagonal(at, n):
            return arena[:, at:at + 64 * n].rearrange("p (k x) -> p k x", x=64)[:, :, 0:64:9]

        psum = ctx.enter_context(nc.psum_tensor("psum", [P, 8, 512], F32))

        sem = lambda name: ctx.enter_context(nc.semaphore(name))
        psum_full = [sem(f"psum_full_{b}") for b in range(8)]
        psum_free = [sem(f"psum_free_{b}") for b in range(8)]
        last_gate_up_loaded = sem("last_gate_up_loaded")
        chunk_loaded = [sem(f"chunk_loaded_{s}") for s in range(2 * RING)]
        x_again = sem("x_again")
        mem_in = [sem("mem_in_0"), sem("mem_in_1")]
        x_in, const_in, gate_in = sem("x_in"), sem("const_in"), sem("gate_in")
        act_step, dve_step = sem("act_step"), sem("dve_step")
        ones_set = sem("ones_set")
        squares = sem("squares")
        root = sem("root")
        mem_normed, x_normed = sem("mem_normed"), sem("x_normed")
        neg_max = sem("neg_max")
        prob_normed = sem("prob_normed")
        q_row_in, q_bcast = sem("q_row_in"), sem("q_bcast")
        kv_in = [sem("kv_in_0"), sem("kv_in_1")]
        k_used, v_used = sem("k_used"), sem("v_used")
        bank7_zero = sem("bank7_zero")
        cache_neg_max, pads_zero = sem("cache_neg_max"), sem("pads_zero")
        eq_built, swish_mid = sem("eq_built"), sem("swish_mid")
        lam_abs, lam_exp, rates = sem("lam_abs"), sem("lam_exp"), sem("rates")
        conv_done, lru_roots_in, lru_roots = sem("conv_done"), sem("lru_roots_in"), sem("lru_roots")
        gelu_in, gelu_tanh, lru_ready = sem("gelu_in"), sem("gelu_tanh"), sem("lru_ready")
        q_rotated, k_rotated = sem("q_rotated"), sem("k_rotated")
        v_row_in, v_bcast = sem("v_row_in"), sem("v_bcast")
        st_in = [sem(f"st_in_{i}") for i in range(3)]
        st_out = [sem(f"st_out_{i}") for i in range(3)]
        st_decayed, st_updated, st_read = sem("st_decayed"), sem("st_updated"), sem("st_read")
        s_out = [sem("s_out_0"), sem("s_out_1")]
        o_normed, g_tanh, ret_ready = sem("o_normed"), sem("g_tanh"), sem("ret_ready")
        branch_merged = sem("branch_merged")
        stored = sem("stored")
        lru_staged, conv_staged = sem("lru_staged"), sem("conv_staged")
        x2_normed, rows_zero, tables_set = sem("x2_normed"), sem("rows_zero"), sem("tables_set")
        row_high, row_rest, row_mid, row_low = sem("row_high"), sem("row_rest"), sem("row_mid"), sem("row_low")
        logitsT_full, logitsT_ready = sem("logitsT_full"), sem("logitsT_ready")
        router_exp_in, router_exp = sem("router_exp_in"), sem("router_exp")
        routed = sem("routed")
        onehot_built, gather_full, scatterT_full = sem("onehot_built"), sem("gather_full"), sem("scatterT_full")
        tokens_ready, scatterT_ready = sem("tokens_ready"), sem("scatterT_ready")
        gate_up_full, gate_tanh, hid_ready = sem("gate_up_full"), sem("gate_tanh"), sem("hid_ready")
        hidT_full, hidT_ready = sem("hidT_full"), sem("hidT_ready")
        y_full, y_ready = sem("y_full"), sem("y_ready")
        scatter_full, scatter_added = sem("scatter_full"), sem("scatter_added")
        tiles03_used, down01_used = sem("tiles03_used"), sem("down01_used")
        pool_out = sem("pool_out")
        final_normed, final_sum, final_root = sem("final_normed"), sem("final_sum"), sem("final_root")
        onehot16_built = sem("onehot16_built")
        row_full, logits_full, masks_ready, ranks_full = sem("row_full"), sem("logits_full"), sem("masks_ready"), sem("ranks_full")

        def states_stored(eng):
            for i in range(3):
                eng.wait_ge(st_out[i], 16 * len(range(i, 2 * NS, 3)))
            for i in range(2):
                eng.wait_ge(s_out[i], 16 * HEADS)

        def full(eng, task):
            b, n = where[task]
            eng.wait_ge(psum_full[b], n + 1)

        def read(eng, task):
            b, n = where[task]
            eng.wait_ge(psum_free[b], n + 1)

        def ps(task):
            return psum[:, where[task][0], :]

        def free_of(task):
            b, n = where[task]
            return psum_free[b], n + 1

        SQUARES = 4 + HEADS
        last = {k: (k, n - 1) for k, n in (("mk", 8), ("mv", 8), ("mq", 8), ("ux", 8), ("uy", 8), ("q", 8), ("k", 8),
                                            ("v", 16), ("ga", 8), ("gb", 8), ("gc", 8))}
        n_state = lambda s: (s // 2, s % 2)

        def router_products(pe):
            for k in range(KT):
                pe.wait_ge(x2_normed, k + 1)
                mm = pe.matmul(psum[0:NLOG, 3, 0:T], rout[:, k, :], xnT[:, k, :], start=k == 0, stop=k == KT - 1)
            mm.then_inc(logitsT_full, 1)
            for u in range(2 * TT):
                t, k4 = divmod(u, 2)
                n = min(P, T - t * P)
                if u >= 2:
                    pe.wait_ge(row_high, u - 1)
                for k in range(4):
                    mm = pe.transpose(psum[0:n, u % 2, k * P:(k + 1) * P], xnT[:, 4 * k4 + k, t * P:t * P + n], ident)
                mm.then_inc(row_full, 1)
                if u == 1:
                    pe.wait_ge(logitsT_ready, 1)
                    for s in range(TT):
                        m = min(P, T - s * P)
                        mm = pe.transpose(psum[0:m, 2, s * 64:s * 64 + NLOG], lgT[0:NLOG, s * P:s * P + m],
                                          ident[0:NLOG, 0:NLOG])
                    mm.then_inc(logits_full, 1)
            pe.wait_ge(masks_ready, 1)
            pe.wait_ge(tables_set, 2)
            for t in range(TT):
                for s in range(t):
                    pe.matmul(psum[:, 3, t * 64:t * 64 + EXPERTS], ones16, M01[:, s, :], start=s == 0, stop=False)
                pe.matmul(psum[:, 3, t * 64:t * 64 + EXPERTS], before16, M01[:, t, :], start=t == 0, stop=True)
            for s in range(TT):
                mm = pe.matmul(psum[:, 3, 192:192 + EXPERTS], ones16, M01[:, s, :], start=s == 0, stop=s == TT - 1)
            mm.then_inc(ranks_full, 1)

        def gather(pe, g, half):
            pe.wait_ge(onehot_built, g + (2 - half))
            if not (isinstance(g, int) and g == 0):
                pe.wait_ge(tokens_ready, g)
            for k in range(KT):
                for t in range(TT):
                    for x in range(3):
                        mm = pe.matmul(psum[:, 0, k * SLOTS:(k + 1) * SLOTS], xr[x][:, t, k * P:(k + 1) * P],
                                       Sb[:, t, half * SLOTS:(half + 1) * SLOTS],
                                       start=t == 0 and x == 0, stop=t == TT - 1 and x == 2)
            mm.then_inc(gather_full, 1)

        def scatter_matrix(pe, e0):
            pe.wait_ge(scatterT_ready, e0 + 2)
            for t in range(TT):
                n = min(P, T - t * P)
                mm = pe.transpose(psum[:, 1, t * P:t * P + n], Sw[0:n, t, :], ident[0:n, 0:n])
            mm.then_inc(scatterT_full, 2)

        def expert_loaded(pe, e0, s, half, beyond=False):
            first = 0 if s >= RING else 16 * ring_uses[s]
            if s < 4 and beyond:
                first -= 16
            pe.wait_ge(chunk_loaded[s], 8 * e0 + (first + 16))

        def gate_up(pe, e0, half, beyond=False):
            base = RING if half == 0 else 0
            pe.wait_ge(tokens_ready, e0 + (half + 1))
            pe.wait_ge(hid_ready, e0 + (half + 1))
            for k in range(KT):
                s = base + 2 * (k // 4)
                early = isinstance(e0, int) and half == 1
                if early:
                    pe.wait_ge(last_gate_up_loaded, 64)
                elif k % 4 == 0:
                    for i in range(2):
                        expert_loaded(pe, e0, s + i, half, beyond)
                w = last_gate_up[:, 2 * (k // 4):2 * (k // 4) + 2, :] if early else slot[:, s:s + 2, :]
                w = w.rearrange("p a (k n) -> p a k n", k=4)[:, :, k % 4, :]
                for a in range(2):
                    mm = pe.matmul(psum[64 * a:64 * a + SLOTS, 2, :], XgT[:, half, k, :],
                                   w[:, :, 256 * a:256 * a + 256], start=k == 0, stop=k == KT - 1)
                if k == 3:
                    mm.then_inc(tiles03_used, 1)
            mm.then_inc(gate_up_full, 1)

        def hidden_T(pe, e):
            pe.wait_ge(hid_ready, e + 2)
            pe.wait_ge(hidT_ready, e + 1)
            for j in range(2):
                mm = pe.transpose(psum[:, 3, j * P:(j + 1) * P], hid[:, j * P:(j + 1) * P], ident)
            mm.then_inc(hidT_full, 1)

        def down(pe, e0):
            pe.wait_ge(hidT_ready, e0 + 3)
            pe.wait_ge(y_ready, e0 + 2)
            for f in range(4):
                if f % 2 == 0:
                    for half in range(2):
                        expert_loaded(pe, e0, (RING if half == 0 else 0) + 4 + f // 2, half)
                for dh in range(2):
                    for half in range(2):
                        w = slot[:, (RING if half == 0 else 0) + 4 + f // 2, :].rearrange("p (k n) -> p k n", k=2)
                        mm = pe.matmul(psum[64 * half:64 * half + SLOTS, 4 + dh, :], hT[:, half, f % 2, f // 2, :],
                                       w[:, f % 2, dh * 512:(dh + 1) * 512], start=f == 0, stop=f == 3)
                if f == 1:
                    mm.then_inc(down01_used, 2)
            mm.then_inc(y_full, 2)

        def scatter(pe, e0):
            pe.wait_ge(y_ready, e0 + 2)
            pe.wait_ge(scatterT_ready, e0 + 2)
            for d in range(KT):
                pe.wait_ge(scatter_added, e0 * 4 + (d + 1))
                pe.matmul(psum[:, 6 + d % 2, 0:T], yS[:, d * P:(d + 1) * P], SwT, start=True,
                          stop=True).then_inc(scatter_full, 1)

        def pair_products(pe, e0, beyond=False, more=True):
            gate_up(pe, e0, 0)
            gather(pe, e0 + 1, 1)
            scatter(pe, e0)
            scatter_matrix(pe, e0)
            hidden_T(pe, e0)
            gate_up(pe, e0, 1, beyond)
            if more:
                gather(pe, e0 + 2, 0)
            hidden_T(pe, e0 + 1)
            down(pe, e0)

        block = ctx.enter_context(nc.Block())

        @block.sync
        def _(sp):
            for h in range(2):
                sp.dma_start(memT[:, 4 * h:4 * h + 4], dram["memT"].rearrange("(k p) n -> p k n", p=P)[:, 4 * h:4 * h + 4]).then_inc(mem_in[h], 16)
            sp.dma_start(const, dram["const"][:, NROPE + NMASK:]).then_inc(const_in, 16)
            sp.dma_start(chan, dram["chan"]).then_inc(const_in, 16)
            sp.dma_start(slot[:, 0, :].rearrange("p (k n) -> p k n", k=KT), chunks[0]).then_inc(chunk_loaded[0], 16)
            sp.dma_start(xT[:], dram["xT"].rearrange("(k p) n -> p k n", p=P)).then_inc(x_in, 16)
            for n in range(1, NCH):
                if n == 8:
                    sp.dma_start(wr, dram["w_r"].rearrange("n c d -> c n d")).then_inc(gate_in, 16)
                    sp.dma_start(wi, dram["w_i"].rearrange("n c d -> c n d")).then_inc(gate_in, 16)
                    sp.dma_start(sconv, dram["sconv"].rearrange("p (k j b) -> p k j b", k=KT, j=3)).then_inc(gate_in, 16)
                    sp.dma_start(slru, dram["slru"].rearrange("p (k b) -> p k b", k=KT)).then_inc(gate_in, 16)
                    sp.dma_start(rout, dram["router"].rearrange("(k p) n -> p k n", p=P)).then_inc(gate_in, 16)
                    sp.dma_start(rbias[0:NLOG, 0:1], dram["rbias"]).then_inc(gate_in, 16)
                    sp.dma_start(buf("rope"), dram["const"][:, 0:NROPE]).then_inc(gate_in, 16)
                    sp.dma_start(buf("dmask"), dram["const"][:, NROPE:NROPE + NMASK]).then_inc(gate_in, 16)
                if n == chunk_of[("ret_out", 0)]:
                    states_stored(sp)
                    full(sp, ("mem_out", KT - 1))
                    sp.dma_start(x_res[:], dram["xT"].rearrange("(k p) n -> p k n", p=P)).then_inc(x_again, 16)
                if n >= RING1:
                    full(sp, last_task[n - RING1])
                sp.dma_start(slot[:, n % RING1, :].rearrange("p (k n) -> p k n", k=KT), chunks[n]).then_inc(
                    chunk_loaded[n % RING1], 16)

            wg = dram["w_gate"].rearrange("g e (k p) f -> (g e) p k f", p=P)
            wu = dram["w_up"].rearrange("g e (k p) f -> (g e) p k f", p=P)
            wd = dram["w_down"].rearrange("g e (k p) d -> (g e) p k d", p=P)

            def expert_part(e, i):
                w = (wg, wu, wg, wu, wd, wd)[i]
                if i < 4:
                    lo = 4 * (i // 2)
                    return w[bass.ds(e, 1), :, lo:lo + 4, :].rearrange("a p k f -> p (a k) f")
                lo = 2 * (i - 4)
                return w[bass.ds(e, 1), :, lo:lo + 2, :].rearrange("a p k f -> p (a k) f")

            def into(s, i):
                return slot[:, s, :].rearrange("p (k n) -> p k n", k=4 if i < 4 else 2)

            sp.wait_ge(ret_ready, VT)
            states_stored(sp)
            for i in range(6):
                sp.dma_start(into(RING + i, i), expert_part(0, i)).then_inc(chunk_loaded[RING + i], 16)
            for i in range(6):
                if i < RING1:
                    full(sp, last_task[max(n for n in range(NCH) if n % RING1 == i)])
                sp.dma_start(into(i, i), expert_part(1, i)).then_inc(chunk_loaded[i], 16)
            for i in range(4):
                sp.dma_start(last_gate_up[:, i, :].rearrange("p (k n) -> p k n", k=4),
                             expert_part(EXPERTS - 1, i)).then_inc(last_gate_up_loaded, 16)
            part_used = (tiles03_used, tiles03_used, gate_up_full, gate_up_full, down01_used, y_full)

            def load_expert(e0, half, e, parts=range(6)):
                base = RING if half == 0 else 0
                for i in parts:
                    sp.wait_ge(part_used[i], e0 + (half - 1) if i < 4 else e0)
                    sp.dma_start(into(base + i, i), expert_part(e, i)).then_inc(chunk_loaded[base + i], 16)

            with sp.Fori(1, EXPERTS // 2 - 1) as pair:
                e0 = sp.snap(pair * 2)
                for half in range(2):
                    load_expert(e0, half, sp.snap(pair * 2 + half))
            load_expert(EXPERTS - 2, 0, EXPERTS - 2)
            load_expert(EXPERTS - 2, 1, EXPERTS - 1, range(4, 6))
            sp.wait_ge(routed, 1)
            end = sp.value_load(ints[0:1, 0:1], min_val=EXPERTS, max_val=EXPERTS + OVER)
            with sp.If(end > EXPERTS):
                with sp.Fori(EXPERTS, end, 2) as e0:
                    for half in range(2):
                        e = sp.value_load(ints[0:1, bass.ds(e0 + (half + 8 - EXPERTS), 1)], min_val=0,
                                          max_val=EXPERTS - 1)
                        load_expert(e0, half, e)
            with sp.Else():
                sp.nop()
            sp.nop()
            for q in range(4):
                sp.wait_ge(final_normed, 2 * q + 2)
                sp.dma_start(outs["y"].rearrange("(k p) n -> p k n", p=P)[:, 2 * q:2 * q + 2],
                             y_out[:, 2 * q:2 * q + 2]).then_inc(stored, 16)
            sp.wait_ge(stored, 16 * 4)
            sp.nop()

        @block.gpsimd
        def _(pool):
            n_stored = 0
            sc_src = dram["state_conv"][:, 1:3, :]
            pool.dma_start(outs["conv_keep"], sc_src).then_inc(pool_out, 16)
            n_stored += 1

            def load_kv(n):
                b = n % NS
                src = dram["cache_mem_k" if n < NS else "cache_mem_v"][b].rearrange("(m p) h d -> p m (h d)", p=P)
                pool.dma_start(kv[:, n % 2, :].rearrange("p (m d) -> p m d", m=2), src).then_inc(kv_in[n % 2], 16)

            def q_broadcast(b):
                if b >= 1:
                    pool.wait_ge(q_bcast, b)
                pool.dma_start(mq_row0[0:1, :], mqs_rows[b:b + 1, :]).then_inc(q_row_in, 16)
                pool.wait_ge(q_row_in, 16 * (b + 1))
                if b >= 2:
                    pool.wait_ge(k_used, b - 1)
                nc.gpsimd.partition_broadcast(qb[:, b % 2, :], mq_row0[0:1, :], P).then_inc(q_bcast, 1)

            read(pool, last["mk"])
            pool.dma_start(outs["mem_k"].rearrange("(m p) d -> p m d", p=P), mk_rows).then_inc(pool_out, 16)
            read(pool, last["mv"])
            pool.dma_start(outs["mem_v"].rearrange("(m p) d -> p m d", p=P), mv_rows).then_inc(pool_out, 16)
            n_stored += 2
            pool.wait_ge(x_normed, 1)
            load_kv(0)
            load_kv(1)
            read(pool, ("mqs", 1))
            for b in range(NS):
                q_broadcast(b)
                if b >= 1:
                    pool.wait_ge(k_used, b)
                    load_kv(b + 1)
            pool.wait_ge(k_used, NS)
            load_kv(NS + 1)
            for b in range(2, NS):
                pool.wait_ge(v_used, b - 1)
                load_kv(NS + b)
                if b == 3:
                    pool.wait_ge(conv_staged, 1)
                    pool.dma_start(outs["conv_new"], conv_st).then_inc(pool_out, 16)
                    n_stored += 1
            pool.wait_ge(lru_staged, 1)
            pool.dma_start(outs["lru"], lru_st).then_inc(pool_out, 16)
            n_stored += 1

            def load_state(s):
                b, hp = n_state(s)
                src = dram["state_ret"][b, 2 * hp:2 * hp + 2].rearrange("h (i p) v -> p (h i) v", p=P)
                if s >= 3:
                    pool.wait_ge(st_out[s % 3], 16 * (s // 3))
                    pool.wait_ge(st_read, s - 2)
                pool.dma_start(st[:, s % 3], src).then_inc(st_in[s % 3], 16)

            def v_broadcast(s):
                b, hp = n_state(s)
                if s >= 1:
                    pool.wait_ge(v_bcast, s)
                pool.dma_start(v_row0[0:1, :], vs_rows[b:b + 1, hp * D:(hp + 1) * D]).then_inc(v_row_in, 16)
                pool.wait_ge(v_row_in, 16 * (s + 1))
                if s >= 2:
                    pool.wait_ge(st_updated, s - 1)
                nc.gpsimd.partition_broadcast(vb[:, s % 2, :], v_row0[0:1, :], P).then_inc(v_bcast, 1)

            read(pool, ("vs", 3))
            read(pool, ("scT",))
            pool.wait_ge(lru_ready, 1)
            load_state(0)
            load_state(1)
            load_state(2)
            v_broadcast(0)
            v_broadcast(1)
            for s in range(2 * NS):
                b, hp = n_state(s)
                pool.wait_ge(st_updated, s + 1)
                dst = outs["ret_s"][b, 2 * hp:2 * hp + 2].rearrange("h (i p) v -> p (h i) v", p=P)
                pool.dma_start(dst, st[:, s % 3]).then_inc(st_out[s % 3], 16)
                if s + 2 < 2 * NS:
                    v_broadcast(s + 2)
                    if s >= 1:
                        load_state(s + 2)
            states_stored(pool)
            pool.wait_ge(pool_out, 16 * n_stored)

            G = nc.gpsimd
            full(pool, ("x2", KT - 1))
            for x in xr:
                G.memset(x[:, 2, :], 0.0).then_inc(rows_zero, 1)
            G.memset(ones16, 1.0).then_inc(tables_set, 1)
            G.tensor_copy(before16, k_("before")).then_inc(tables_set, 1)
            for u in range(2 * TT + 1):
                if u < 2 * TT:
                    t, k4 = divmod(u, 2)
                    n, c = min(P, T - t * P), slice(512 * k4, 512 * k4 + 512)
                    pool.wait_ge(row_high, u + 1)
                    if u >= 2:
                        pool.wait_ge(row_mid, u - 1)
                        pool.wait_ge(row_low, u - 1)
                    G.tensor_tensor(xres[0:n, u % 2, :], xrow[0:n, u % 2, :], xr[0][0:n, t, c],
                                    ALU.subtract).then_inc(row_rest, 1)
                if u >= 1:
                    t, k4 = divmod(u - 1, 2)
                    n, c = min(P, T - t * P), slice(512 * k4, 512 * k4 + 512)
                    pool.wait_ge(row_mid, u)
                    G.tensor_tensor(xr[2][0:n, t, c], xres[0:n, (u - 1) % 2, :], xr[1][0:n, t, c],
                                    ALU.subtract).then_inc(row_low, 1)
            G.memset(filler[:, 0:8], 0.0).then_inc(hid_ready, 1)
            G.memset(filler[:, 8:16], 0.0).then_inc(hidT_ready, 1)
            G.memset(filler[:, 16:24], 0.0).then_inc(scatter_added, 2)
            G.memset(SwT, 0.0).then_inc(scatterT_ready, 2)
            G.memset(yS, 0.0).then_inc(y_ready, 2)

        @block.tensor
        def _(pe):
            def begin(task):
                b, n = where[task]
                if n >= 1:
                    pe.wait_ge(psum_free[b], n)

            def end(task, mm):
                mm.then_inc(psum_full[where[task][0]], 1)

            def loaded(n):
                pe.wait_ge(chunk_loaded[n % RING1], 16 * (n // RING1 + 1))

            def weights(n):
                return slot[:, n % RING1, :].rearrange("p (k n) -> p k n", k=KT)

            def project(task, rhs, ready=None):
                kind, i = task
                n = chunk_of[(kind, i // 2)]
                loaded(n)
                begin(task)
                w = weights(n)
                two = kind == "ret_out"
                for k in range(KT):
                    if ready:
                        pe.wait_ge(ready[0], ready[1] + k + 1)
                    mm = pe.matmul(ps(task)[:, 0:T], w[:, k, (i % 2) * P:(i % 2 + 1) * P], rhs[:, k, :],
                                   start=k == 0, stop=k == KT - 1 and not two)
                if two:
                    n += 1
                    loaded(n)
                    w = weights(n)
                    for k in range(KT):
                        if ready:
                            pe.wait_ge(ready[0], ready[1] + KT + k + 1)
                        mm = pe.matmul(ps(task)[:, 0:T], w[:, k, (i % 2) * P:(i % 2 + 1) * P], rhs[:, KT + k, :],
                                       start=False, stop=k == KT - 1)
                end(task, mm)

            def column_sums(task, src, n, cols, first=None):
                begin(task)
                for k in range(n):
                    if first is not None and k % 4 == 0:
                        pe.wait_ge(squares, first + k // 4)
                    mm = pe.matmul(ps(task)[:, 0:cols], ones, src[:, k, 0:cols], start=k == 0, stop=k == n - 1)
                end(task, mm)

            def residual_squares(k):
                pe.wait_ge(squares, SQUARES + k + 1)
                return pe.matmul(ps(("x2_sq",))[:, 0:T], ones, sq3[:, k, :], start=k == 0, stop=k == KT - 1)

            rhs_of = {"mq": xnT, "ux": xnT, "uy": xnT, "q": xnT, "k": xnT, "v": xnT, "g": xnT, "ga": xnT,
                      "gb": xnT, "gc": xnT, "lru_out": uyT, "ret_out": oT, "mem_out": cT, "x2": merged}
            pe.wait_ge(ones_set, 1)
            for task in order:
                kind = task[0]
                if kind in NO_PSUM:
                    continue
                if kind == "mem_sq":
                    column_sums(task, sq, KT, TP, 1)
                    pe.wait_ge(const_in, 32)
                elif kind == "x_sq":
                    column_sums(task, sq, KT, T, 3)
                elif kind in ("mk", "mv"):
                    i = task[1]
                    n = chunk_of[(kind, i // 2)]
                    loaded(n)
                    begin(task)
                    w = weights(n)
                    m = i % 2
                    for k in range(KT):
                        if task == ("mk", 0):
                            pe.wait_ge(mem_normed, k + 1)
                        mm = pe.matmul(ps(task)[:, 0:256], memT[:, k, m * P:(m + 1) * P], w[:, k, :],
                                       start=k == 0, stop=k == KT - 1)
                    end(task, mm)
                elif kind in rhs_of:
                    if task == ("mq", 0):
                        pe.wait_ge(x_normed, 1)
                    if task == ("lru_out", 0):
                        pe.wait_ge(lru_ready, 1)
                    if task == ("mem_out", 0):
                        read(pe, ("pv", 3, 1))
                        read(pe, ("scT",))
                    if task == ("x2", 0):
                        begin(("x2_sq",))
                    project(task, rhs_of[kind], {("ret_out", 0): (ret_ready, 0), ("x2", 0): (branch_merged, KT)}.get(task))
                    if kind == "x2" and task[1] >= 2:
                        residual_squares(task[1] - 2)
                elif kind == "mkT":
                    q = task[1]
                    read(pe, last["mk"])
                    begin(task)
                    for k in range(2):
                        for m in range(2):
                            mm = pe.transpose(ps(task)[:, (2 * k + m) * P:(2 * k + m + 1) * P],
                                              mk_rows[:, m, (2 * q + k) * P:(2 * q + k + 1) * P], ident)
                    end(task, mm)
                elif kind == "mqs":
                    read(pe, last["mq"])
                    begin(task)
                    for k in range(4):
                        mm = pe.transpose(ps(task)[0:NS, k * P:(k + 1) * P], mqT[:, 4 * task[1] + k, TP:T], ident)
                    end(task, mm)
                elif kind == "lg":
                    _, h, l = task
                    read(pe, ("mkT", 3))
                    read(pe, last["mq"])
                    begin(task)
                    for i in range(2):
                        mm = pe.matmul(ps(task)[:, 0:TP], mqT[:, 2 * h + i, l * P:(l + 1) * P], mkT[:, 2 * h + i, :],
                                       start=i == 0, stop=i == 1)
                    end(task, mm)
                elif kind == "pT":
                    h = task[1]
                    pe.wait_ge(prob_normed, 2 * h + 2)
                    begin(task)
                    for m in range(2):
                        for l in range(2):
                            mm = pe.transpose(ps(task)[:, (2 * m + l) * P:(2 * m + l + 1) * P],
                                              prob[:, h % 2, l, m * P:(m + 1) * P], ident)
                    end(task, mm)
                elif kind == "pv":
                    _, h, j = task
                    read(pe, ("pT", h))
                    begin(task)
                    for m in range(2):
                        mm = pe.matmul(ps(task)[:, 0:TP], mv_rows[:, m, (2 * h + j) * P:(2 * h + j + 1) * P],
                                       probT[:, m, :], start=m == 0, stop=m == 1)
                    end(task, mm)
                elif kind in ("r", "i"):
                    n = task[1]
                    pe.wait_ge(conv_done, 1)
                    pe.wait_ge(gate_in, 16 * 8)
                    begin(task)
                    end(task, pe.matmul(ps(task)[:, 0:T], (wr if kind == "r" else wi)[:, n, :], uc[:, n, :],
                                        start=True, stop=True))
                elif kind == "kr":
                    _, m, q = task
                    pe.wait_ge(k_rotated, 1)
                    begin(task)
                    for k in range(4):
                        mm = pe.transpose(ps(task)[:, k * P:(k + 1) * P], kT[:, 4 * q + k, m * P:(m + 1) * P], ident)
                    end(task, mm)
                elif kind == "sl":
                    pe.wait_ge(k_used, NS)
                    begin(task)
                    for m in range(2):
                        mm = pe.transpose(ps(task)[0:32, m * P:(m + 1) * P], L[:, 32 * m:32 * m + 32], ident)
                    end(task, mm)
                elif kind == "spT":
                    pe.wait_ge(prob_normed, 2 * HEADS + 1)
                    begin(task)
                    for m in range(2):
                        mm = pe.transpose(ps(task)[:, m * 32:m * 32 + 32], p32[0:32, m * P:(m + 1) * P],
                                          ident[0:32, 0:32])
                    end(task, mm)
                elif kind == "sc":
                    b = task[1]
                    if b == 0:
                        read(pe, ("spT",))
                        pe.wait_ge(bank7_zero, 1)
                    n = NS + b
                    pe.wait_ge(kv_in[n % 2], 16 * (n // 2 + 1))
                    for m in range(2):
                        for h in range(HEADS):
                            mm = pe.matmul(psum[32 * h:32 * h + NS, 7, 0:DK], PM[:, m, h, b, :],
                                           kv[:, n % 2, m * D + h * DK:m * D + (h + 1) * DK],
                                           start=b == 0 and m == 0, stop=b == NS - 1 and m == 1)
                    mm.then_inc(v_used, 1)
                elif kind == "scT":
                    read(pe, ("sc", NS - 1))
                    begin(task)
                    for j in range(2):
                        mm = pe.transpose(ps(task)[:, j * P:(j + 1) * P], cs[:, j * P:(j + 1) * P], ident)
                    end(task, mm)
                elif kind == "vs":
                    read(pe, last["v"])
                    begin(task)
                    for k in range(4):
                        mm = pe.transpose(ps(task)[0:NS, k * P:(k + 1) * P], vT[:, 4 * task[1] + k, TP:T], ident)
                    end(task, mm)
                elif kind == "vr":
                    _, m, q = task
                    begin(task)
                    for k in range(4):
                        mm = pe.transpose(ps(task)[:, k * P:(k + 1) * P], vT[:, 4 * q + k, m * P:(m + 1) * P], ident)
                    end(task, mm)
                elif kind == "att":
                    h = task[1]
                    pe.wait_ge(q_rotated, 1)
                    begin(task)
                    for i in range(2):
                        pe.matmul(ps(task)[:, 0:TP], kT[:, 2 * h + i, 0:P], qT[:, 2 * h + i, 0:TP],
                                  start=i == 0, stop=i == 1)
                    for i in range(2):
                        mm = pe.matmul(ps(task)[:, TP:TP + P], kT[:, 2 * h + i, P:TP], qT[:, 2 * h + i, P:TP],
                                       start=i == 0, stop=i == 1)
                    end(task, mm)
                elif kind == "o":
                    _, h, j = task
                    if j == 0:
                        read(pe, ("att", h))
                        read(pe, ("vr", 1, 3))
                    begin(task)
                    c = h * DV + j * P
                    pe.matmul(ps(task)[:, 0:TP], v_rows[:, 0, c:c + P], attT[:, 0:TP], start=True, stop=False)
                    end(task, pe.matmul(ps(task)[:, P:TP], v_rows[:, 1, c:c + P], attT[:, TP:TP + P],
                                        start=False, stop=True))
                elif kind == "S":
                    _, h, i = task
                    if i == 0:
                        read(pe, ("kr", 1, 1))
                    begin(task)
                    for m in range(2):
                        mm = pe.matmul(ps(task)[:, 0:DV], k_rows[:, m, (2 * h + i) * P:(2 * h + i + 1) * P],
                                       v_rows[:, m, h * DV:(h + 1) * DV], start=m == 0, stop=m == 1)
                    end(task, mm)
                elif kind == "so":
                    s = task[1]
                    b, hp = n_state(s)
                    if s == 0:
                        pe.wait_ge(bank7_zero, 2)
                    pe.wait_ge(st_updated, s + 1)
                    for i in range(2):
                        for h2 in range(2):
                            h = 2 * hp + h2
                            mm = pe.matmul(psum[32 * h:32 * h + NS, 7, :], QM[:, 2 * h + i, b, :],
                                           st[:, s % 3, 2 * h2 + i, :],
                                           start=b == 0 and i == 0, stop=b == NS - 1 and i == 1)
                    mm.then_inc(st_read, 1)
                elif kind == "soT":
                    read(pe, ("so", 0))
                    begin(task)
                    for j in range(4):
                        mm = pe.transpose(ps(task)[:, j * P:(j + 1) * P], os_[:, j * P:(j + 1) * P], ident)
                    end(task, mm)
                elif kind == "on":
                    pe.wait_ge(squares, 5 + task[1])
                    column_sums(task, sq2[:, task[1] % 2], 4, T)
                elif kind == "x2_sq":
                    residual_squares(KT - 2)
                    end(task, residual_squares(KT - 1))
                else:
                    raise AssertionError(kind)

            router_products(pe)
            pe.wait_ge(row_low, 2 * TT)
            gather(pe, 0, 0)
            with pe.Fori(0, EXPERTS - 2, 2) as e0:
                pair_products(pe, e0)
            pair_products(pe, EXPERTS - 2, more=False)
            end = pe.value_load(ints[0:1, 0:1], min_val=EXPERTS, max_val=EXPERTS + OVER)
            with pe.If(end > EXPERTS):
                gather(pe, EXPERTS, 0)
                with pe.Fori(EXPERTS, end, 2) as e0:
                    pair_products(pe, e0, beyond=True)
            with pe.Else():
                pe.nop()
            pe.nop()
            scatter(pe, end)
            for k in range(KT):
                pe.wait_ge(squares, SQUARES + KT + k + 1)
                mm = pe.matmul(psum[:, 0, 0:T], ones, sq3[:, k, :], start=k == 0, stop=k == KT - 1)
            mm.then_inc(final_sum, 1)

        @block.scalar
        def _(act):
            steps = Steps(act, act_step)

            def run(out, in_, func, sem=None, **kw):
                steps.did(nc.scalar.activation(out, in_, func, **kw), sem)

            def norm_root(task, cols, slot_, width):
                full(act, task)
                run(rstd[:, slot_, 0:cols], ps(task)[:, 0:cols], ACT.Sqrt, free_of(task), scale=1.0 / width,
                    bias=eps_col[:, 0:1])

            act.wait_ge(ones_set, 2)
            for task in order:
                kind = task[0]
                if kind == "mem_sq":
                    for q in range(2):
                        act.wait_ge(mem_in[q], 16)
                        run(sq[:, 4 * q:4 * q + 4, 0:TP], memT[:, 4 * q:4 * q + 4, :], ACT.Square, squares)
                    norm_root(task, TP, 0, D)
                elif kind == "xq":
                    act.wait_ge(x_in, 16)
                    for q in range(2):
                        run(sq[:, 4 * q:4 * q + 4, :], xT[:, 4 * q:4 * q + 4, :], ACT.Square, squares)
                elif kind == "x_sq":
                    norm_root(task, T, 1, D)
                elif kind == "lam":
                    act.wait_ge(lam_abs, 1)
                    run(small[:, 0:KT], small[:, 0:KT], ACT.Exp, lam_exp, scale=-1.0)
                elif kind in ("mk", "mv"):
                    i = task[1]
                    full(act, task)
                    dst = mk_rows if kind == "mk" else mv_rows
                    run(dst[:, i % 2, (i // 2) * 256:(i // 2 + 1) * 256], ps(task)[:, 0:256], ACT.Copy, free_of(task))
                elif kind in ("mq", "uy", "q", "v", "ux"):
                    i = task[1]
                    full(act, task)
                    if task == ("ux", 0):
                        act.wait_ge(pads_zero, 1)
                        act.wait_ge(pool_out, 16 * 3)
                    dst = {"mq": mqT, "uy": uyT, "q": qT, "v": vT, "ux": uxp}[kind]
                    lo = 3 if kind == "ux" else 0
                    run(dst[:, i, lo:lo + T], ps(task)[:, 0:T], ACT.Copy, free_of(task))
                elif kind == "k":
                    full(act, task)
                    run(kT[:, task[1], :], ps(task)[:, 0:T], ACT.Copy, free_of(task), scale=DK ** -0.5)
                elif kind == "mkT":
                    q = task[1]
                    full(act, task)
                    run(mkT[:, 2 * q:2 * q + 2, :], ps(task).rearrange("p (k n) -> p k n", k=2), ACT.Copy, free_of(task))
                elif kind == "mqs":
                    full(act, task)
                    run(mqs_rows[0:NS, 512 * task[1]:512 * task[1] + 512], ps(task)[0:NS, :], ACT.Copy, free_of(task))
                elif kind == "lg":
                    _, h, l = task
                    act.wait_ge(neg_max, 2 * h + l + 1)
                    if h >= 2:
                        full(act, ("pT", h - 2))
                    run(prob[:, h % 2, l, :], ps(task)[:, 0:TP], ACT.Exp, free_of(task), scale=DK ** -0.5,
                        bias=stats[:, 2 * h + l:2 * h + l + 1], accum_out=stats[:, 8 + 2 * h + l:9 + 2 * h + l])
                elif kind == "pT":
                    h = task[1]
                    full(act, task)
                    if h >= 1:
                        full(act, ("pv", h - 1, 1))
                    run(probT, ps(task).rearrange("p (m l) -> p m l", m=2), ACT.Copy, free_of(task))
                elif kind == "pv":
                    _, h, j = task
                    full(act, task)
                    run(cT[:, 2 * h + j, 0:TP], ps(task)[:, 0:TP], ACT.Copy, free_of(task))
                elif kind in ("r", "i"):
                    n = task[1]
                    full(act, task)
                    act.wait_ge(rates, 1)
                    dst = (Tr if kind == "r" else Ti)[:, n, :]
                    col = n if kind == "r" else KT + n
                    run(dst, ps(task)[:, 0:T], ACT.Tanh, free_of(task), scale=0.5, bias=brh[:, col:col + 1])
                    if kind == "r":
                        steps.settle()
                        run(dst, dst, ACT.Tanh, scale=sp4[:, n:n + 1], bias=sp4[:, n:n + 1])
                elif kind == "lru_root":
                    act.wait_ge(lru_roots_in, 1)
                    run(Rb, Rb, ACT.Sqrt, lru_roots, scale=2.0, bias=eps_col[:, 1:2])
                    run(Tr, Tr, ACT.Sqrt, lru_roots)
                elif kind == "gelu_tanh":
                    act.wait_ge(gelu_in, 1)
                    run(Ti, Ti, ACT.Tanh, gelu_tanh, scale=float(np.sqrt(2.0 / np.pi)))
                elif kind == "kr":
                    _, m, q = task
                    full(act, task)
                    for h2 in range(2):
                        h = 2 * q + h2
                        c = HEADS * m + h
                        run(k_rows[:, m, 256 * h:256 * h + 256], ps(task)[:, 256 * h2:256 * h2 + 256], ACT.Copy,
                            free_of(task) if h2 else None, scale=k_("kdec")[:, c:c + 1])
                elif kind == "sl":
                    act.wait_ge(cache_neg_max, 1)
                    run(p32[0:32, :], ps(task)[0:32, 0:TP], ACT.Exp, free_of(task), scale=DK ** -0.5,
                        bias=stats[0:32, 16:17], accum_out=stats[0:32, 17:18])
                elif kind == "sc" and task[1] == NS - 1:
                    act.wait_ge(v_used, NS)
                    run(cs, psum[:, 7, 0:TP], ACT.Copy, psum_free[7])
                elif kind == "vs":
                    full(act, task)
                    q = task[1]
                    run(vs_rows[0:NS, 512 * q:512 * q + 512], ps(task)[0:NS, :], ACT.Copy, free_of(task))
                elif kind == "vr":
                    _, m, q = task
                    full(act, task)
                    run(v_rows[:, m, 512 * q:512 * q + 512], ps(task), ACT.Copy, free_of(task))
                elif kind in ("ga", "gb", "gc"):
                    i = task[1]
                    full(act, task)
                    if kind == "gb":
                        act.wait_ge(branch_merged, i + 1)
                    run((merged if kind == "ga" else tgate)[:, i, :], ps(task)[:, 0:T], ACT.Tanh, free_of(task), scale=0.5)
                elif kind == "sd":
                    s = task[1]
                    b, hp = n_state(s)
                    act.wait_ge(st_in[s % 3], 16 * (s // 3 + 1))
                    for h2 in range(2):
                        v = st[:, s % 3, 2 * h2:2 * h2 + 2, :]
                        run(v, v, ACT.Copy, st_decayed, scale=GAMMA[2 * hp + h2])
                elif kind == "so" and task[1] == 2 * NS - 1:
                    act.wait_ge(st_read, 2 * NS)
                    run(os_, psum[:, 7, :], ACT.Copy, psum_free[7])
                elif kind == "o":
                    _, h, j = task
                    full(act, task)
                    run(oT[:, 4 * h + j, 0:TP], ps(task)[:, 0:TP], ACT.Copy, free_of(task))
                elif kind == "S":
                    _, h, i = task
                    n = 2 * h + i
                    full(act, task)
                    if n >= 2:
                        act.wait_ge(s_out[n % 2], 16 * (n // 2))
                    run(S_st[:, n % 2, :], ps(task), ACT.Copy, free_of(task))
                    steps.settle()
                    act.dma_start(outs["ret_p"][h, i * P:(i + 1) * P, :], S_st[:, n % 2, :]).then_inc(s_out[n % 2], 16)
                elif kind == "oq":
                    h = task[1]
                    if h == 0:
                        read(act, ("soT",))
                        states_stored(act)
                    if h >= 2:
                        full(act, ("on", h - 2))
                    run(sq2[:, h % 2], oT[:, 4 * h:4 * h + 4, :], ACT.Square, squares)
                elif kind == "on":
                    h = task[1]
                    full(act, task)
                    if h >= 2:
                        act.wait_ge(o_normed, h - 1)
                    run(rstd[:, h % 2, :], ps(task)[:, 0:T], ACT.Sqrt, free_of(task), scale=4.0 / DV, bias=eps_col[:, 2:3])
                elif kind == "g":
                    i = task[1]
                    full(act, task)
                    if i >= 2:
                        act.wait_ge(ret_ready, i - 1)
                    run(gt[:, i % 2, :], ps(task)[:, 0:T], ACT.Tanh, g_tanh, scale=0.5)
                elif kind == "x2":
                    read(act, task)
                    run(sq3[:, task[1], :], x_res[:, task[1], :], ACT.Square, squares)
                elif kind == "x2_sq":
                    norm_root(task, T, 0, D)

            def rows_of(u):
                t, k4 = divmod(u, 2)
                return min(P, T - t * P), t, slice(512 * k4, 512 * k4 + 512)

            for u in range(2 * TT + 1):
                if u < 2 * TT:
                    n, t, c = rows_of(u)
                    act.wait_ge(row_full, u + 1)
                    if u == 2 * (TT - 1):
                        act.wait_ge(rows_zero, 3)
                    if u >= 2:
                        act.wait_ge(row_rest, u - 1)
                    run(xrow[0:n, u % 2, :], psum[0:n, u % 2, :], ACT.Copy)
                    run(xr[0][0:n, t, c], psum[0:n, u % 2, :], ACT.Copy, row_high)
                if u >= 1:
                    n, t, c = rows_of(u - 1)
                    act.wait_ge(row_rest, u)
                    run(xr[1][0:n, t, c], xres[0:n, (u - 1) % 2, :], ACT.Copy, row_mid)
                if u == 2:
                    act.wait_ge(router_exp_in, 1)
                    run(tmpB[:, 0:TT * 8], tmpB[:, 0:TT * 8], ACT.Exp, router_exp)

            def take_tokens(g, half):
                act.wait_ge(gather_full, g + 1)
                run(XgT[:, half, :, :], psum[:, 0, :].rearrange("p (k s) -> p k s", k=KT), ACT.Copy, tokens_ready)

            def chunk_tanh(e):
                act.wait_ge(gate_up_full, e + 1)
                act.wait_ge(hid_ready, e + 1)
                run(tg, psum[:, 2, 0:256], ACT.Tanh, gate_tanh, scale=0.5)

            def chunk_hidden(e, half):
                act.wait_ge(hidT_full, e + 1)
                run(hT[:, half], psum[:, 3, 0:256].rearrange("p (j a s) -> p j a s", j=2, a=2), ACT.Copy, hidT_ready)

            def pair_copies(e0, more=True):
                chunk_tanh(e0)
                take_tokens(e0 + 1, 1)
                act.wait_ge(scatterT_full, e0 + 2)
                nc.scalar.activation(SwT, psum[:, 1, 0:T], ACT.Copy).then_inc(scatterT_ready, 2)
                chunk_hidden(e0, 0)
                chunk_tanh(e0 + 1)
                if more:
                    take_tokens(e0 + 2, 0)
                chunk_hidden(e0 + 1, 1)
                act.wait_ge(y_full, e0 + 2)
                nc.scalar.activation(yS, psum[:, 4:6, :], ACT.Copy).then_inc(y_ready, 2)

            take_tokens(0, 0)
            with act.Fori(0, EXPERTS - 2, 2) as e0:
                pair_copies(e0)
            pair_copies(EXPERTS - 2, more=False)
            end = act.value_load(ints[0:1, 0:1], min_val=EXPERTS, max_val=EXPERTS + OVER)
            with act.If(end > EXPERTS):
                take_tokens(EXPERTS, 0)
                with act.Fori(EXPERTS, end, 2) as e0:
                    pair_copies(e0)
            with act.Else():
                act.nop()
            act.nop()
            for d in range(KT):
                act.wait_ge(scatter_added, end * 4 + (d + 3))
                nc.scalar.activation(sq3[:, d, :], x_res[:, d, :], ACT.Square).then_inc(squares, 1)
            act.wait_ge(final_sum, 1)
            run(rstd[:, 0, :], psum[:, 0, 0:T], ACT.Sqrt, final_root, scale=1.0 / D, bias=eps_col[:, 0:1])

        @block.vector
        def _(dve):
            V = nc.vector
            steps = Steps(dve, dve_step)
            did, settle = steps.did, steps.settle

            def v(instruction, sem=None):
                did(instruction, sem)
                settle()

            def bc(ap, shape):
                return ap.to_broadcast(list(shape))

            v(V.memset(ones, 1.0), ones_set)
            v(V.memset(eps_col[:, 0:1], EPS))
            v(V.memset(eps_col[:, 1:2], -1.0))
            v(V.memset(eps_col[:, 2:3], 4 * EPS), ones_set)
            dve.wait_ge(const_in, 32)
            for task in order:
                kind = task[0]
                if kind == "mem_sq":
                    read(dve, task)
                    v(V.reciprocal(rstd[:, 0, 0:TP], rstd[:, 0, 0:TP]))
                    for k in range(KT):
                        did(V.scalar_tensor_tensor(memT[:, k, :], memT[:, k, :], cv("norm_mem", k), rstd[:, 0, 0:TP],
                                                   ALU.mult, ALU.mult), mem_normed)
                elif kind == "lam":
                    lam, y, s_, s2, c_, t_ = (small[:, 8 * i:8 * i + 8] for i in (7, 0, 1, 2, 3, 4))
                    v(V.tensor_scalar(lam, cvs("lam"), -1.0, None, ALU.mult))
                    v(V.tensor_tensor(y, lam, cvs("lam"), ALU.max), lam_abs)
                    v(V.tensor_scalar(brh[:, 0:2 * KT], chan[:, CH["b_r"] * KT:(CH["b_i"] + 1) * KT], 0.5, None, ALU.mult))
                    dve.wait_ge(lam_exp, 1)
                    v(V.tensor_scalar(t_, y, 2.0, None, ALU.add))
                    v(V.reciprocal(t_, t_))
                    v(V.tensor_tensor(s_, y, t_, ALU.mult))
                    v(V.tensor_tensor(s2, s_, s_, ALU.mult))
                    v(V.tensor_scalar(c_, s2, 1.0 / 15.0, None, ALU.mult))
                    for n in (13, 11, 9, 7, 5, 3):
                        v(V.scalar_tensor_tensor(c_, c_, 1.0 / n, s2, ALU.add, ALU.mult))
                    v(V.scalar_tensor_tensor(c_, c_, 1.0, s_, ALU.add, ALU.mult))
                    v(V.tensor_scalar(lam, lam, 0.0, 4.0, ALU.max, ALU.mult))
                    v(V.scalar_tensor_tensor(sp4, c_, 8.0, lam, ALU.mult, ALU.add), rates)
                elif kind == "x_sq":
                    dve.wait_ge(x_in, 16)
                    read(dve, task)
                    v(V.reciprocal(rstd[:, 1, :], rstd[:, 1, :]))
                    for k in range(KT):
                        did(V.scalar_tensor_tensor(xnT[:, k, :], xT[:, k, :], cv("norm_mix", k), rstd[:, 1, :],
                                                   ALU.mult, ALU.mult), x_normed if k == KT - 1 else None)
                elif task == ("mqs", 0):
                    full(dve, task)
                    did(V.memset(uxp[:, :, 0:3], 0.0), pads_zero)
                elif kind == "lg":
                    _, h, l = task
                    full(dve, task)
                    c = stats[:, 2 * h + l:2 * h + l + 1]
                    v(V.tensor_reduce(c, ps(task)[:, 0:TP], AX.X, ALU.max, negate=True))
                    v(V.tensor_scalar(c, c, DK ** -0.5, None, ALU.mult), neg_max)
                    if l == 1:
                        for l in range(2):
                            read(dve, ("lg", h, l))
                            c = stats[:, 8 + 2 * h + l:9 + 2 * h + l]
                            v(V.reciprocal(c, c))
                            v(V.tensor_scalar(prob[:, h % 2, l, :], prob[:, h % 2, l, :], c, None, ALU.mult), prob_normed)
                elif kind == "conv":
                    read(dve, last["ux"])
                    dve.wait_ge(gate_in, 16 * 8)
                    did(V.tensor_copy(conv_st, uxp[:, :, TP:TP + 11]), conv_staged)
                    for j in (3, 2, 1, 0):
                        for k in range(KT):
                            src, dst = uxp[:, k, j:j + TP], uc[:, k, 0:TP]
                            if j == 3:
                                did(V.tensor_scalar(dst, src, cv("w3", k), cv("conv_b", k), ALU.mult, ALU.add))
                            else:
                                did(V.scalar_tensor_tensor(dst, src, cv(f"w{j}", k), dst, ALU.mult, ALU.add))
                        settle()
                    us, ut = uc[:, :, TP:T], tiles(convt, KT)
                    shape = (P, KT, NS)
                    v(V.tensor_tensor(us, uxp[:, :, 3 + TP:3 + T], bc(cvs("w3").unsqueeze(2), shape), ALU.mult))
                    v(V.tensor_tensor(us, us, bc(cvs("conv_b").unsqueeze(2), shape), ALU.add))
                    for j in range(3):
                        v(V.tensor_tensor(ut, sconv[:, :, j, :], bc(cvs(f"w{j}").unsqueeze(2), shape), ALU.mult))
                        v(V.tensor_tensor(us, us, ut, ALU.add), conv_done if j == 2 else None)
                elif kind == "kl":
                    b = task[1]
                    dve.wait_ge(q_bcast, b + 1)
                    dve.wait_ge(kv_in[b % 2], 16 * (b // 2 + 1))
                    v(V.tensor_tensor(prod.rearrange("p (m d) -> p m d", m=2),
                                      kv[:, b % 2, :].rearrange("p (m d) -> p m d", m=2),
                                      bc(qb[:, b % 2, :].unsqueeze(1), (P, 2, D)), ALU.mult))
                    v(V.tensor_reduce(L.rearrange("p (m b h) -> p m b h", m=2, b=NS)[:, :, b, :],
                                      prod.rearrange("p (m h d) -> p m h d", m=2, h=HEADS), AX.X, ALU.add), k_used)
                elif kind == "lru":
                    read(dve, ("i", KT - 1))
                    v(V.tensor_scalar(Rb, Tr, 1.0, None, ALU.add))
                    v(V.reciprocal(Rb, Rb))
                    v(V.scalar_tensor_tensor(Tr, Tr, 0.5, Rb, ALU.mult, ALU.mult))
                    v(V.scalar_tensor_tensor(Ti, Ti, 1.0, uc, ALU.add, ALU.mult))
                    v(V.tensor_scalar(Rb, Rb, 0.5, None, ALU.max), lru_roots_in)
                    dve.wait_ge(lru_roots, 2)
                    v(V.memset(Tr[:, :, 0:1], 0.5))
                    v(V.tensor_tensor(Ti, Tr, Ti, ALU.mult))
                    for k in range(KT):
                        did(V.tensor_tensor_scan(Tr[:, k, 0:TP], Rb[:, k, 0:TP], Ti[:, k, 0:TP], 0.0, ALU.mult, ALU.add))
                    v(V.tensor_tensor(Tr[:, :, TP:T], Rb[:, :, TP:T], slru, ALU.mult))
                    v(V.tensor_tensor(Tr[:, :, TP:T], Tr[:, :, TP:T], Ti[:, :, TP:T], ALU.add))
                    v(V.tensor_copy(lru_st, Tr[:, :, TP - 1:T]), lru_staged)
                elif kind == "gelu":
                    read(dve, last["uy"])
                    v(V.tensor_tensor(Ti, uyT, uyT, ALU.mult))
                    v(V.tensor_scalar(Ti, Ti, 0.044715, 1.0, ALU.mult, ALU.add))
                    v(V.tensor_tensor(Ti, Ti, uyT, ALU.mult), gelu_in)
                    dve.wait_ge(gelu_tanh, 1)
                    v(V.scalar_tensor_tensor(uyT, Ti, 1.0, uyT, ALU.add, ALU.mult))
                    v(V.scalar_tensor_tensor(uyT, uyT, 0.5, Tr, ALU.mult, ALU.mult), lru_ready)
                elif kind in ("rot_q", "rot_k"):
                    x = (qT if kind == "rot_q" else kT).rearrange("p (h i) t -> p h i t", i=2)
                    x1, x2_ = x[:, :, 0, :], x[:, :, 1, :]
                    t1, t2 = (rtmp[:, i * HEADS * T:(i + 1) * HEADS * T].rearrange("p (h t) -> p h t", h=HEADS) for i in (0, 1))
                    cos, sin = (bc(k_(n).unsqueeze(1), (P, HEADS, T)) for n in ("cos", "sin"))
                    read(dve, last["q" if kind == "rot_q" else "k"])
                    full(dve, ("i", KT - 1))
                    v(V.tensor_tensor(t1, x2_, sin, ALU.mult))
                    v(V.tensor_tensor(t2, x1, sin, ALU.mult))
                    v(V.tensor_tensor(x1, x1, cos, ALU.mult))
                    v(V.tensor_tensor(x2_, x2_, cos, ALU.mult))
                    v(V.tensor_tensor(x1, x1, t1, ALU.subtract))
                    v(V.tensor_tensor(x2_, x2_, t2, ALU.add), q_rotated if kind == "rot_q" else k_rotated)
                    if kind == "rot_q":
                        v(V.memset(QM, 0.0))
                        v(V.tensor_copy(diagonal(QMd, KT), qT[:, :, TP:T]))
                elif kind == "sl":
                    full(dve, ("i", KT - 1))
                    v(V.memset(buf("PM"), 0.0))
                    v(V.memset(psum[:, 7, :], 0.0), bank7_zero)
                    full(dve, task)
                    c = stats[0:32, 16:17]
                    v(V.tensor_reduce(c, ps(task)[0:32, 0:TP], AX.X, ALU.max, negate=True))
                    v(V.tensor_scalar(c, c, DK ** -0.5, None, ALU.mult), cache_neg_max)
                    read(dve, task)
                    v(V.reciprocal(stats[0:32, 17:18], stats[0:32, 17:18]))
                    v(V.tensor_scalar(p32[0:32, :], p32[0:32, :], stats[0:32, 17:18], None, ALU.mult), prob_normed)
                elif kind == "spT":
                    full(dve, task)
                    for m in range(2):
                        v(V.tensor_copy(diagonal(PMd + 256 * m, HEADS),
                                        ps(task)[:, 32 * m:32 * m + 32].rearrange("p (b h) -> p h b", h=HEADS)),
                          free_of(task) if m else None)
                elif kind == "scT":
                    full(dve, task)
                    for j in range(2):
                        v(V.tensor_copy(cT.rearrange("p (h j) t -> p h j t", j=2)[:, :, j, TP:T],
                                        ps(task)[:, j * P:(j + 1) * P].rearrange("p (h b) -> p h b", h=HEADS)[:, :, 0:NS]),
                          free_of(task) if j else None)
                    v(V.memset(psum[:, 7, :], 0.0), bank7_zero)
                elif kind == "att":
                    h = task[1]
                    full(dve, task)
                    if h >= 1:
                        full(dve, ("o", h - 1, 3))
                    v(V.tensor_tensor(attT, ps(task)[:, 0:384], k_("dmask")[:, 384 * h:384 * h + 384], ALU.mult),
                      free_of(task))
                elif kind == "sd":
                    s = task[1]
                    b, hp = n_state(s)
                    dve.wait_ge(v_bcast, s + 1)
                    dve.wait_ge(st_decayed, 2 * s + 2)
                    for h2 in range(2):
                        for i in range(2):
                            x = st[:, s % 3, 2 * h2 + i, :]
                            did(V.scalar_tensor_tensor(x, vb[:, s % 2, h2 * DV:(h2 + 1) * DV],
                                                       kT[:, 2 * (2 * hp + h2) + i, TP + b:TP + b + 1], x,
                                                       ALU.mult, ALU.add), st_updated if h2 and i else None)
                elif kind == "soT":
                    full(dve, task)
                    for h in range(HEADS):
                        did(V.tensor_copy(oT[:, 4 * h:4 * h + 4, TP:T],
                                          ps(task).rearrange("p (j c) -> p j c", j=4)[:, :, 32 * h:32 * h + NS]),
                            free_of(task) if h == HEADS - 1 else None)
                elif kind == "on":
                    h = task[1]
                    read(dve, task)
                    r = rstd[:, h % 2, :]
                    v(V.reciprocal(r, r))
                    x = oT[:, 4 * h:4 * h + 4, :]
                    v(V.tensor_tensor(x, x, bc(r.unsqueeze(1), (P, 4, T)), ALU.mult), o_normed)
                elif kind == "g":
                    i = task[1]
                    dve.wait_ge(g_tanh, i + 1)
                    x = gt[:, i % 2, :]
                    v(V.scalar_tensor_tensor(x, x, 1.0, ps(task)[:, 0:T], ALU.add, ALU.mult), free_of(task))
                    v(V.tensor_tensor(oT[:, i, :], oT[:, i, :], x, ALU.mult), ret_ready)
                elif kind == "lru_out":
                    i = task[1]
                    full(dve, task)
                    read(dve, ("ga", i))
                    v(V.scalar_tensor_tensor(merged[:, i, :], merged[:, i, :], 1.0, ps(task)[:, 0:T], ALU.add, ALU.mult),
                      free_of(task))
                elif kind in ("ret_out", "mem_out"):
                    i = task[1]
                    full(dve, task)
                    read(dve, ("gb" if kind == "ret_out" else "gc", i))
                    x = tgate[:, i, :]
                    v(V.scalar_tensor_tensor(x, x, 1.0, ps(task)[:, 0:T], ALU.add, ALU.mult), free_of(task))
                    v(V.tensor_tensor(merged[:, i, :], merged[:, i, :], x, ALU.add), branch_merged)
                elif kind == "x2":
                    i = task[1]
                    full(dve, task)
                    dve.wait_ge(x_again, 16)
                    did(V.scalar_tensor_tensor(x_res[:, i, :], ps(task)[:, 0:T], 0.5, x_res[:, i, :], ALU.mult, ALU.add),
                        free_of(task))
                elif kind == "x2_sq":
                    settle()
                    read(dve, task)
                    v(V.reciprocal(rstd[:, 0, :], rstd[:, 0, :]))
                    for k in range(KT):
                        did(V.scalar_tensor_tensor(xnT[:, k, :], x_res[:, k, :], cv("norm_ffn", k), rstd[:, 0, :],
                                                   ALU.mult, ALU.mult), x2_normed)

            settle()
            states_stored(dve)
            v(V.memset(lgt, 0.0))
            v(V.memset(Rc, -1.0))
            v(V.memset(Wc, 0.0))
            dve.wait_ge(logitsT_full, 1)
            v(V.tensor_scalar(lgT[0:NLOG, :], psum[0:NLOG, 3, 0:T], rbias[0:NLOG, 0:1], None, ALU.add), logitsT_ready)

            dve.wait_ge(logits_full, 1)
            lgp = psum[:, 2, 0:192].rearrange("p (t c) -> p t c", t=TT)
            v(V.tensor_copy(lgt[:, 0:2, :], lgp[:, 0:2, 0:NLOG]))
            v(V.tensor_copy(lgt[0:T - 2 * P, 2:3, :], lgp[0:T - 2 * P, 2:3, 0:NLOG]))
            G, E8 = GROUPS, PER_GROUP
            c32, c8 = k_("count32"), k_("count8")

            def view(base, at, n):
                return base[:, at:at + TT * n].rearrange("p (t n) -> p t n", t=TT)

            def first_max(onehot, peak, x, n, scratch):
                v(V.tensor_reduce(peak, x, AX.X, ALU.max))
                v(V.tensor_tensor(onehot, x, bc(peak, (P, TT, n)), ALU.is_lt))
                v(V.scalar_tensor_tensor(onehot, onehot, 64.0, bc(c32[:, 0:n].unsqueeze(1), (P, TT, n)), ALU.mult, ALU.add))
                v(V.tensor_reduce(scratch, onehot, AX.X, ALU.min))
                v(V.tensor_tensor(onehot, onehot, bc(scratch, (P, TT, n)), ALU.is_equal))

            oh_g, oh_1, oh_2 = view(tmpC, 0, G), view(tmpC, 16, E8), view(tmpC, 48, E8)
            peak, pos, sel = view(tmpC, 80, 1), view(tmpC, 84, 1), view(tmpC, 96, E8)
            sel2, gs, w1, w2, sgm = view(tmpC, 128, E8), view(tmpC, 160, 1), view(tmpC, 164, 1), view(tmpC, 168, 1), view(tmpC, 172, 1)
            pk1, pk2 = view(tmpC, 176, 1), view(tmpC, 180, 1)
            lg_g = lgt[:, :, 0:G]
            ex = view(tmpB, 0, 8)
            first_max(oh_g, peak, lg_g, G, pos)
            v(V.tensor_tensor(ex[:, :, 0:G], lg_g, bc(peak, (P, TT, G)), ALU.subtract))
            for g in range(G):
                src = lgt[:, :, G + g * E8:G + (g + 1) * E8]
                if g == 0:
                    v(V.tensor_tensor(sel, src, bc(oh_g[:, :, 0:1], (P, TT, E8)), ALU.mult))
                else:
                    v(V.tensor_tensor(sel2, src, bc(oh_g[:, :, g:g + 1], (P, TT, E8)), ALU.mult))
                    v(V.tensor_tensor(sel, sel, sel2, ALU.add))
            first_max(oh_1, pk1, sel, E8, pos)
            v(V.scalar_tensor_tensor(sel2, oh_1, -3.0e38, sel, ALU.mult, ALU.add))
            first_max(oh_2, pk2, sel2, E8, pos)
            v(V.tensor_tensor(ex[:, :, 4:5], pk2, pk1, ALU.subtract))
            v(V.memset(ex[:, :, 5:8], 0.0), router_exp_in)
            dve.wait_ge(router_exp, 1)
            v(V.tensor_reduce(gs, ex[:, :, 0:G], AX.X, ALU.add))
            v(V.tensor_scalar(sgm, ex[:, :, 4:5], 1.0, 2.0, ALU.add, ALU.mult))
            v(V.tensor_tensor(gs, gs, sgm, ALU.mult))
            v(V.reciprocal(w1, gs))
            v(V.tensor_tensor(w2, w1, ex[:, :, 4:5], ALU.mult))
            v(V.tensor_tensor(sel, oh_1, oh_2, ALU.add))
            v(V.tensor_tensor(sel, sel, bc(k_("valid").unsqueeze(2), (P, TT, E8)), ALU.mult))
            v(V.tensor_tensor(oh_1, oh_1, bc(w1, (P, TT, E8)), ALU.mult))
            v(V.tensor_tensor(oh_2, oh_2, bc(w2, (P, TT, E8)), ALU.mult))
            v(V.tensor_tensor(sel2, oh_1, oh_2, ALU.add))
            for g in range(G):
                v(V.tensor_tensor(M01[:, :, g * E8:(g + 1) * E8], sel, bc(oh_g[:, :, g:g + 1], (P, TT, E8)), ALU.mult),
                  masks_ready if g == G - 1 else None)
            for g in range(G):
                v(V.tensor_tensor(Wc[:, :, g * E8:(g + 1) * E8], sel2, bc(oh_g[:, :, g:g + 1], (P, TT, E8)), ALU.mult))
            dve.wait_ge(ranks_full, 1)
            rkp = psum[:, 3, 0:192].rearrange("p (t c) -> p t c", t=TT)[:, :, 0:EXPERTS]
            R32 = tmpD[:, 0:TT * EXPERTS].rearrange("p (t e) -> p t e", t=TT)
            v(V.scalar_tensor_tensor(R32, rkp, 1.0, M01, ALU.add, ALU.mult))
            v(V.tensor_scalar(Rc[:, :, 0:EXPERTS], R32, -1.0, None, ALU.add))
            def build(g):
                if not (isinstance(g, int) and g == 0):
                    dve.wait_ge(scatterT_full, g)
                    dve.wait_ge(onehot16_built, g)
                    dve.wait_ge(onehot_built, g)
                col = slice(g, g + 2) if isinstance(g, int) else bass.ds(g, 2)
                sh4 = (P, TT, 2, SLOTS)
                four = lambda x: x.rearrange("p t (a s) -> p t a s", a=2)
                V.tensor_tensor(four(eq), bc(k_("slot").unsqueeze(1).unsqueeze(1), sh4),
                                bc(Rc[:, :, col].unsqueeze(3), sh4), ALU.is_equal).then_inc(eq_built, 2)
                dve.wait_ge(eq_built, g + 2)
                V.tensor_copy(Sb, eq).then_inc(onehot16_built, 2)
                V.tensor_tensor(four(Sw), four(eq), bc(Wc[:, :, col].unsqueeze(3), sh4), ALU.mult).then_inc(
                    onehot_built, 2)

            def hidden(e):
                dve.wait_ge(gate_tanh, e + 1)
                V.scalar_tensor_tensor(tmid, tg, 1.0, psum[:, 2, 0:256], ALU.add, ALU.mult).then_inc(swish_mid, 1)
                dve.wait_ge(swish_mid, e + 1)
                V.tensor_tensor(hid, tmid, psum[:, 2, 256:512], ALU.mult).then_inc(hid_ready, 1)

            def add_scattered(e0):
                for d in range(KT):
                    dve.wait_ge(scatter_full, e0 * 4 + (d + 1))
                    V.tensor_tensor(x_res[:, d, :], x_res[:, d, :], psum[:, 6 + d % 2, 0:T], ALU.add).then_inc(
                        scatter_added, 1)

            def pair_vectors(e0):
                hidden(e0)
                dve.wait_ge(scatter_added, e0 * 4 + 2)
                add_scattered(e0)
                build(e0 + 2)
                hidden(e0 + 1)

            settle()
            build(0)
            dve.wait_ge(onehot_built, 2)
            cnt, ext, cum, exc, tm = (ov[:, 32 * i:32 * i + 32] for i in range(5))
            ej, cx, vj, kj = (ov[:, 160 + 8 * i:168 + 8 * i] for i in range(4))
            big = tmpA[:, 0:OVER * EXPERTS].rearrange("p (j e) -> p j e", j=OVER)
            oh_j = tmpA[:, OVER * EXPERTS:2 * OVER * EXPERTS].rearrange("p (j e) -> p j e", j=OVER)
            sh = (P, OVER, EXPERTS)
            v(V.tensor_copy(cnt, psum[:, 3, 192:192 + EXPERTS]))
            v(V.tensor_scalar(ext, cnt, float(SLOTS), None, ALU.is_gt))
            for k in range(2, (T - 1) // SLOTS + 1):
                v(V.tensor_scalar(tm, cnt, float(SLOTS * k), None, ALU.is_gt))
                v(V.tensor_tensor(ext, ext, tm, ALU.add))
            v(V.tensor_tensor_scan(cum, ones[:, 0:EXPERTS], ext, 0.0, ALU.mult, ALU.add))
            v(V.tensor_tensor(exc, cum, ext, ALU.subtract))
            v(V.tensor_tensor(big, bc(cum.unsqueeze(1), sh), bc(c8.unsqueeze(2), sh), ALU.is_le))
            v(V.tensor_reduce(ej, big, AX.X, ALU.add))
            v(V.tensor_tensor(oh_j, bc(c32.unsqueeze(1), sh), bc(ej.unsqueeze(2), sh), ALU.is_equal))
            v(V.tensor_tensor(big, oh_j, bc(exc.unsqueeze(1), sh), ALU.mult))
            v(V.tensor_reduce(cx, big, AX.X, ALU.add))
            v(V.tensor_tensor(kj, c8, cx, ALU.subtract))
            v(V.tensor_scalar(kj, kj, float(SLOTS), float(SLOTS + 1), ALU.mult, ALU.add))
            for t in range(TT):
                v(V.tensor_tensor(big, oh_j, bc(R32[:, t:t + 1, :], sh), ALU.mult))
                v(V.tensor_reduce(vj, big, AX.X, ALU.add))
                v(V.tensor_tensor(Rc[:, t, EXPERTS:EXPERTS + OVER], vj, kj, ALU.subtract))
                v(V.tensor_tensor(big, oh_j, bc(Wc[:, t:t + 1, 0:EXPERTS], sh), ALU.mult))
                v(V.tensor_reduce(Wc[:, t, EXPERTS:EXPERTS + OVER], big, AX.X, ALU.add))
            v(V.tensor_scalar(ej, ej, float(EXPERTS - 1), None, ALU.min))
            v(V.tensor_copy(ints[:, 8:16], ej))
            v(V.tensor_tensor(vj, c8, bc(cum[:, EXPERTS - 1:EXPERTS], (P, OVER)), ALU.is_lt))
            v(V.tensor_reduce(kj[:, 0:1], vj[:, 0:OVER:2], AX.X, ALU.add))
            v(V.tensor_scalar(kj[:, 0:1], kj[:, 0:1], 2.0, float(EXPERTS), ALU.mult, ALU.add))
            v(V.tensor_copy(ints[:, 0:1], kj[:, 0:1]), routed)
            with dve.Fori(0, EXPERTS - 2, 2) as e0:
                pair_vectors(e0)
            pair_vectors(EXPERTS - 2)
            end = dve.value_load(ints[0:1, 0:1], min_val=EXPERTS, max_val=EXPERTS + OVER)
            with dve.If(end > EXPERTS):
                with dve.Fori(EXPERTS, end, 2) as e0:
                    pair_vectors(e0)
            with dve.Else():
                dve.nop()
            dve.nop()
            dve.wait_ge(scatter_added, end * 4 + 2)
            add_scattered(end)
            dve.wait_ge(final_root, 1)
            V.reciprocal(rstd[:, 0, :], rstd[:, 0, :]).then_inc(final_root, 1)
            dve.wait_ge(final_root, 2)
            for k in range(KT):
                V.scalar_tensor_tensor(y_out[:, k, :], x_res[:, k, :], cv("norm_final", k), rstd[:, 0, :],
                                       ALU.mult, ALU.mult).then_inc(final_normed, 1)


_OUTS = {
    "y": (D, T), "conv_keep": (NS, 2, D), "conv_new": (P, KT, 11), "lru": (P, KT, 9),
    "ret_p": (HEADS, DK, DV), "ret_s": (NS, HEADS, DK, DV), "mem_k": (TP, D), "mem_v": (TP, D),
}


def kernel(**inputs):
    import concourse.bacc as bacc
    from concourse.bass_utils import run_bass_kernel_spmd

    x = {k: np.asarray(v) for k, v in inputs.items()}
    f = np.ascontiguousarray
    cols = lambda a: a.reshape(KT, P).T
    names = ["norm_mix", "norm_ffn", "norm_mem", None, "conv_b", "b_r", "b_i", "lru_lambda"]
    chan = [cols(x[n][0]) if n else cols(x["norm_final"]) for n in names]
    chan += [cols(x["conv_w"][0, j]) for j in range(4)]
    const, const_at = shape_constants()
    arrays = {
        "const": const,
        "chan": f(np.concatenate(chan, axis=1)),
        "xT": f(np.concatenate([x["x_prompt"][0], x["x_sample"][:, 0]], axis=0).T),
        "memT": f(x["mem_prompt"][0].T),
        "sconv": f(x["state_conv"][0].reshape(NS, 3, KT, P).transpose(3, 2, 1, 0).reshape(P, -1)),
        "slru": f(x["state_lru"][0].reshape(NS, KT, P).transpose(2, 1, 0).reshape(P, -1)),
        "router": f(np.concatenate([x["w_grp"][0], x["w_exp_router"][0].transpose(1, 0, 2).reshape(D, EXPERTS)], axis=1)),
        "rbias": f(np.concatenate([x["b_grp"][0], x["b_exp_router"][0].reshape(-1)])[:, None]),
        "state_conv": x["state_conv"][0], "state_ret": x["state_ret"][0],
        "cache_mem_k": x["cache_mem_k"][0], "cache_mem_v": x["cache_mem_v"][0],
    }
    for n in ("w_in", "w_mem_kv", "w_r", "w_i", "w_branch_lru", "w_branch_ret", "w_branch_mem", "w_out", "w_gate",
              "w_up", "w_down"):
        arrays[n] = x[n][0]
    nc = bacc.Bacc("TRN2", target_bir_lowering=False, num_devices=1)
    dram = {n: nc.dram_tensor(f"in_{n}", a.shape, F32, kind="ExternalInput").ap() for n, a in arrays.items()}
    outs = {n: nc.dram_tensor(f"out_{n}", s, F32, kind="ExternalOutput").ap() for n, s in _OUTS.items()}
    build_program(nc, dram, outs, const_at)
    r = run_bass_kernel_spmd(nc, [{f"in_{n}": a for n, a in arrays.items()}], core_ids=[0]).results[0]
    o = {n: np.asarray(r[f"out_{n}"]) for n in _OUTS}
    y = o["y"].T
    rows = lambda a: a.transpose(2, 1, 0).reshape(a.shape[2], D)
    conv, lru = rows(o["conv_new"]), rows(o["lru"])
    conv_s = np.concatenate([o["conv_keep"], conv[3:, None, :]], axis=1)
    return (f(y[:TP])[None], f(y[TP:])[:, None], f(conv[:3])[None, None], f(lru[:1])[None], o["ret_p"][None, None],
            o["mem_k"].reshape(1, 1, TP, HEADS, DK), o["mem_v"].reshape(1, 1, TP, HEADS, DK), f(conv_s)[None],
            f(lru[1:])[None], o["ret_s"][None])
```
